# Optimizing a Trainium2 kernel written in Bass

```python
import math
import jax, jax.numpy as jnp
from jax import lax
import numpy as np

D_MODEL = 1024
BATCH = 1
SEQ = 512
DEPTH = 2

N_MIXERS = 2
HEAD_DIM = 64
SWA_Q_HEADS = D_MODEL // HEAD_DIM
SWA_KV_HEADS = SWA_Q_HEADS // 4
SWA_GROUP = SWA_Q_HEADS // SWA_KV_HEADS
SWA_WINDOW = 128
FOX_HEADS = D_MODEL // HEAD_DIM
BLOCK = 128
ROPE_THETA = 500000.0
ROT_DIM = HEAD_DIM // 4
N_EXPERTS = 16
N_GROUPS = 4
EXPERTS_PER_GROUP = N_EXPERTS // N_GROUPS
TOP_K = 2
D_EXPERT = D_MODEL // 4
ALPHA = (2.0 * DEPTH) ** 0.25
BETA = (8.0 * DEPTH) ** -0.25
LN_EPS = 1e-5
NEG = -1e30
N_SWA_LAYERS = (DEPTH + 1) // 2
N_FOX_LAYERS = DEPTH // 2
SWA_IN = (SWA_Q_HEADS + 2 * SWA_KV_HEADS) * HEAD_DIM
FOX_IN = 3 * FOX_HEADS * HEAD_DIM + FOX_HEADS

kernel_name = "hybrid_swa_sink_fox_deepnorm_group_moe"

def layer_norm(x, gain, bias):
    xf = x.astype(jnp.float32)
    mu = jnp.mean(xf, axis=-1, keepdims=True)
    var = jnp.mean(jnp.square(xf - mu), axis=-1, keepdims=True)
    y = (xf - mu) * lax.rsqrt(var + LN_EPS)
    return (y * gain.astype(jnp.float32) + bias.astype(jnp.float32)).astype(x.dtype)

def partial_rope(x, pos):
    half = ROT_DIM // 2
    inv_freq = jnp.power(ROPE_THETA, -jnp.arange(half, dtype=jnp.float32) * (2.0 / ROT_DIM))
    ang = pos.astype(jnp.float32)[:, None] * inv_freq[None, :]
    cos = jnp.cos(ang)[None, :, None, :]
    sin = jnp.sin(ang)[None, :, None, :]
    xr = x[..., :ROT_DIM].astype(jnp.float32)
    x1, x2 = xr[..., :half], xr[..., half:]
    rot = jnp.concatenate([x1 * cos - x2 * sin, x2 * cos + x1 * sin], axis=-1).astype(x.dtype)
    return jnp.concatenate([rot, x[..., ROT_DIM:]], axis=-1)

def swa_sink_attention(x, w_in, sinks, w_o):
    B, S, _ = x.shape
    nb = S // BLOCK
    qd, kd = SWA_Q_HEADS * HEAD_DIM, SWA_KV_HEADS * HEAD_DIM
    proj = x @ w_in
    q = proj[..., :qd].reshape(B, S, SWA_Q_HEADS, HEAD_DIM)
    k = proj[..., qd:qd + kd].reshape(B, S, SWA_KV_HEADS, HEAD_DIM)
    v = proj[..., qd + kd:].reshape(B, S, SWA_KV_HEADS, HEAD_DIM)
    pos = jnp.arange(S)
    q = partial_rope(q, pos)
    k = partial_rope(k, pos)
    qb = q.reshape(B, nb, BLOCK, SWA_KV_HEADS, SWA_GROUP, HEAD_DIM)

    def with_prev(t):
        tb = t.reshape(B, nb, BLOCK, SWA_KV_HEADS, HEAD_DIM)
        prev = jnp.pad(tb, ((0, 0), (1, 0), (0, 0), (0, 0), (0, 0)))[:, :-1]
        return jnp.concatenate([prev, tb], axis=2)

    kk, vv = with_prev(k), with_prev(v)
    scores = jnp.einsum('bnqhgd,bnshd->bnhgqs', qb, kk).astype(jnp.float32) * (HEAD_DIM ** -0.5)
    q_pos = jnp.arange(nb)[:, None] * BLOCK + jnp.arange(BLOCK)[None, :]
    k_pos = jnp.arange(nb)[:, None] * BLOCK - BLOCK + jnp.arange(2 * BLOCK)[None, :]
    diff = q_pos[:, :, None] - k_pos[:, None, :]
    allowed = (diff >= 0) & (diff < SWA_WINDOW) & (k_pos[:, None, :] >= 0)
    scores = jnp.where(allowed[None, :, None, None], scores, NEG)
    sink = sinks.astype(jnp.float32).reshape(SWA_KV_HEADS, SWA_GROUP)
    sink_col = jnp.broadcast_to(sink[None, None, :, :, None, None], scores.shape[:-1] + (1,))
    probs = jax.nn.softmax(jnp.concatenate([scores, sink_col], axis=-1), axis=-1)[..., :-1]
    out = jnp.einsum('bnhgqs,bnshd->bnqhgd', probs.astype(vv.dtype), vv)
    return out.reshape(B, S, SWA_Q_HEADS * HEAD_DIM) @ w_o

def forgetting_attention(x, w_in, b_f, w_o):
    B, S, _ = x.shape
    hd_all = FOX_HEADS * HEAD_DIM
    proj = x @ w_in
    q = proj[..., :hd_all].reshape(B, S, FOX_HEADS, HEAD_DIM)
    k = proj[..., hd_all:2 * hd_all].reshape(B, S, FOX_HEADS, HEAD_DIM)
    v = proj[..., 2 * hd_all:3 * hd_all].reshape(B, S, FOX_HEADS, HEAD_DIM)
    f_logit = (proj[..., 3 * hd_all:] + b_f).astype(jnp.float32)
    c = jnp.cumsum(jax.nn.log_sigmoid(f_logit), axis=1).transpose(0, 2, 1)
    scale = HEAD_DIM ** -0.5
    outs = []
    for n in range(S // BLOCK):
        q0, end = n * BLOCK, (n + 1) * BLOCK
        s = jnp.einsum('bqhd,bkhd->bhqk', q[:, q0:end], k[:, :end]).astype(jnp.float32) * scale
        s = s + c[:, :, q0:end, None] - c[:, :, None, :end]
        causal = jnp.arange(q0, end)[:, None] >= jnp.arange(end)[None, :]
        p = jax.nn.softmax(jnp.where(causal, s, NEG), axis=-1)
        outs.append(jnp.einsum('bhqk,bkhd->bqhd', p.astype(v.dtype), v[:, :end]))
    out = jnp.concatenate(outs, axis=1).reshape(B, S, hd_all)
    return out @ w_o

def grouped_moe(h, w_router, b_router, w_gate, w_up, w_down):
    B, S, D = h.shape
    h2 = h.reshape(B * S, D)
    T = h2.shape[0]
    logits = (h2 @ w_router).astype(jnp.float32) + b_router.astype(jnp.float32)
    scores = jax.nn.softmax(logits, axis=-1)
    g = scores.reshape(T, N_GROUPS, EXPERTS_PER_GROUP)
    group_score = jnp.sum(lax.top_k(g, TOP_K)[0], axis=-1)
    best = jnp.argmax(group_score, axis=-1)
    in_group = jax.nn.one_hot(best, N_GROUPS, dtype=jnp.bool_)[:, :, None]
    masked = jnp.where(in_group, g, -1.0).reshape(T, N_EXPERTS)
    top_vals, top_idx = lax.top_k(masked, TOP_K)
    gates = top_vals / jnp.sum(top_vals, axis=-1, keepdims=True)
    gate_dense = jnp.sum(jax.nn.one_hot(top_idx, N_EXPERTS, dtype=jnp.float32) * gates[..., None], axis=1)
    hg = jnp.einsum('td,edf->tef', h2, w_gate)
    hu = jnp.einsum('td,edf->tef', h2, w_up)
    act = jax.nn.silu(hg) * hu * gate_dense[:, :, None].astype(h2.dtype)
    y = jnp.einsum('tef,efd->td', act, w_down)
    return y.reshape(B, S, D)

def setup_inputs(seed: int = 0) -> dict:
    key = jax.random.key(seed)
    ks = jax.random.split(key, 20)
    f32 = jnp.float32
    nrm = lambda k, shape, s: jax.random.normal(k, shape, f32) * s
    qk_cols_swa = (SWA_Q_HEADS + SWA_KV_HEADS) * HEAD_DIM
    v_cols_swa = SWA_KV_HEADS * HEAD_DIM
    swa_w_in = jnp.concatenate([
        nrm(ks[1], (N_SWA_LAYERS, D_MODEL, qk_cols_swa), D_MODEL ** -0.5),
        nrm(ks[2], (N_SWA_LAYERS, D_MODEL, v_cols_swa), D_MODEL ** -0.5 * BETA)], axis=-1)
    fox_hd = FOX_HEADS * HEAD_DIM
    fox_w_in = jnp.concatenate([
        nrm(ks[5], (N_FOX_LAYERS, D_MODEL, 2 * fox_hd), D_MODEL ** -0.5),
        nrm(ks[6], (N_FOX_LAYERS, D_MODEL, fox_hd), D_MODEL ** -0.5 * BETA),
        nrm(ks[7], (N_FOX_LAYERS, D_MODEL, FOX_HEADS), 0.5 * D_MODEL ** -0.5)], axis=-1)
    return {
        "x": jax.random.normal(ks[0], (BATCH, SEQ, D_MODEL), f32),
        "ln_gain": 1.0 + nrm(ks[3], (DEPTH, 2, D_MODEL), 0.02),
        "ln_bias": nrm(ks[4], (DEPTH, 2, D_MODEL), 0.02),
        "swa_w_in": swa_w_in,
        "swa_sinks": nrm(ks[8], (N_SWA_LAYERS, SWA_Q_HEADS), 0.5),
        "swa_w_o": nrm(ks[9], (N_SWA_LAYERS, SWA_Q_HEADS * HEAD_DIM, D_MODEL), (SWA_Q_HEADS * HEAD_DIM) ** -0.5 * BETA),
        "fox_w_in": fox_w_in,
        "fox_b_f": jax.random.uniform(ks[10], (N_FOX_LAYERS, FOX_HEADS), f32, 1.0, 6.0),
        "fox_w_o": nrm(ks[11], (N_FOX_LAYERS, fox_hd, D_MODEL), fox_hd ** -0.5 * BETA),
        "w_router": nrm(ks[12], (D_MODEL, N_EXPERTS), D_MODEL ** -0.5),
        "b_router": nrm(ks[13], (N_EXPERTS,), 0.01),
        "w_gate": nrm(ks[14], (DEPTH, N_EXPERTS, D_MODEL, D_EXPERT), D_MODEL ** -0.5),
        "w_up": nrm(ks[15], (DEPTH, N_EXPERTS, D_MODEL, D_EXPERT), D_MODEL ** -0.5),
        "w_down": nrm(ks[16], (DEPTH, N_EXPERTS, D_EXPERT, D_MODEL), D_EXPERT ** -0.5 * BETA),
    }

def reference(x, ln_gain, ln_bias, swa_w_in, swa_sinks, swa_w_o, fox_w_in, fox_b_f, fox_w_o,
              w_router, b_router, w_gate, w_up, w_down):
    for i in range(DEPTH):
        j = i // N_MIXERS
        if i % N_MIXERS == 0:
            mix = swa_sink_attention(x, swa_w_in[j], swa_sinks[j], swa_w_o[j])
        else:
            mix = forgetting_attention(x, fox_w_in[j], fox_b_f[j], fox_w_o[j])
        x = layer_norm(ALPHA * x + mix, ln_gain[i, 0], ln_bias[i, 0])
        ffn = grouped_moe(x, w_router, b_router, w_gate[i], w_up[i], w_down[i])
        x = layer_norm(ALPHA * x + ffn, ln_gain[i, 1], ln_bias[i, 1])
    return x


_drawn_inputs = setup_inputs


def setup_inputs(seed=0):
    import zlib

    import numpy as np

    out = dict(_drawn_inputs(seed))
    spreads = {}
    factors = {'swa_sinks': 7.719}
    for name, (base, spread) in spreads.items():
        noise = np.random.default_rng([zlib.crc32(name.encode()), seed]).standard_normal(out[name].shape)
        drawn = base * np.exp(spread * noise) if base else spread * noise
        out[name] = __import__('jax').numpy.asarray(drawn.astype(out[name].dtype))
    for name, factor in factors.items():
        out[name] = (out[name] * factor).astype(out[name].dtype)
    return out
```

```python
import concourse.bass as bass
from concourse import mybir
from contextlib import ExitStack

P = 128
SEQ, D = 512, 1024
HD = 64
NH = D // HD
NKV = NH // 4
WINDOW = 128
NT = SEQ // P
KC = D // P
BLK = 512
NE, NG, TOPK = 16, 4, 2
EPG = NE // NG
F = D // 4
FC = F // P
ROT = HD // 4
DEPTH = 2
ALPHA = (2.0 * DEPTH) ** 0.25
LN_EPS = 1e-5
SCALE = HD ** -0.5
NEG = -1e30
CAP = P
OVF = SEQ * TOPK // (CAP + 1)
SLOTS = (NE + OVF) * CAP
PAIRS = NH // 2
UNITS = NH * NT
RING = 4
SLOT_WORDS = KC * BLK + FC * D
IN_BLOCKS = (3, 6)
OUT_BLOCKS = 2
IN_USE = (0, IN_BLOCKS[0] + OUT_BLOCKS + NE)
OUT_USE = tuple(IN_USE[l] + IN_BLOCKS[l] for l in range(DEPTH))
EXP_USE = tuple(OUT_USE[l] + OUT_BLOCKS for l in range(DEPTH))


def trunk(nc, x, ln_gain, ln_bias, swa_w_in, swa_sinks, swa_w_o, fox_w_in, fox_b_f, fox_w_o,
          w_router, b_router, w_gate, w_up, w_down, rope, out):
    fp32, i32, u32 = mybir.dt.float32, mybir.dt.int32, mybir.dt.uint32
    ALU = mybir.AluOpType
    ACT = mybir.ActivationFunctionType
    X = mybir.AxisListType.X

    ctx = ExitStack()
    with ctx:
        def sb(name, shape, dt=fp32):
            return ctx.enter_context(nc.sbuf_tensor(name, shape, dt))

        xres = sb("xres", [P, NT, D])
        xT = sb("xT", [P, KC, SEQ])
        ring = sb("ring", [P, RING, SLOT_WORDS])
        lnp = sb("lnp", [P, 2, D])
        ident = sb("ident", [P, P])
        before = sb("before", [P, P])
        ones = sb("ones", [P, P])
        band = sb("band", [P, 2, P])
        causal = sb("causal", [P, P])
        cs = sb("cs", [P, NT, 2, ROT])
        sink = sb("sink", [P, NH])
        wr = sb("wr", [P, KC, NE])
        wf = sb("wf", [P, KC, NH])
        br = sb("br", [P, NE])
        bf = sb("bf", [NH, 1])
        stats = sb("stats", [P, NT, 2, 6])
        mv = sb("mv", [P, NT, 2])
        veps = sb("veps", [P, NT])
        rstd = sb("rstd", [P, NT])
        mhalf = sb("mhalf", [P, NT])
        nmax = sb("nmax", [P, 4])
        nmax1 = sb("nmax1", [P, 4])
        rsum = sb("rsum", [P, 4, 2])
        rinv = sb("rinv", [P, 4, 2])
        gates = sb("gates", [P, NT, 2])
        pos = sb("pos", [P, NT, 2], u32)
        ovf_id = sb("ovf_id", [1, 8], i32)
        arena = sb("arena", [P, 15700])

        def area(at, n, pattern=None, **kw):
            a = arena[:, at:at + n]
            return a.rearrange(pattern, **kw) if pattern else a

        QT = area(0, PAIRS * SEQ, "p (h t) -> p h t", h=PAIRS)
        KT = area(4096, PAIRS * SEQ, "p (h t) -> p h t", h=PAIRS)
        V = area(8192, NT * D, "p (t n) -> p t n", t=NT)
        sp = area(12288, 3 * 516, "p (b n) -> p b n", b=3)
        pT = area(13836, 2 * SEQ, "p (b n) -> p b n", b=2)
        heads = area(14860, 2 * P, "p (b n) -> p b n", b=2)
        rtmp = area(15116, 2 * 8 * ROT, "p (a n) -> p a n", a=2)
        tok = area(6144, 2 * BLK, "p (b n) -> p b n", b=2)
        zeros = area(10240, D)
        xTf = xT[:, :, :].rearrange("p c t -> p (c t)")
        cb = xTf[:, 0:2048].rearrange("p (b h n) -> p b h n", b=2, h=2)
        mb = xTf[:, 2048:4096].rearrange("p (b h n) -> p b h n", b=2, h=2)
        fz = area(12288, 4 * SEQ, "p (k n) -> p k n", k=4)
        def small(at, *shape):
            n = 1
            for s in shape:
                n *= s
            a = area(at, n)
            if len(shape) == 2:
                return a.rearrange("p (a b) -> p a b", a=shape[0])
            if len(shape) == 3:
                return a.rearrange("p (a b c) -> p a b c", a=shape[0], b=shape[1])
            return a
        lg, pr, tmp, msk, oh1, oh2, asn, slot = (small(14000 + 64 * k, NT, NE) for k in range(8))
        prg = area(14064, 64).rearrange("p (t g e) -> p t g e", t=NT, g=NG)
        pair = small(14512, NT, NG, 6)
        gs, gk = small(14608, NT, NG), small(14624, NT, NG)
        red = small(14640, 12, NT)
        cnt, ext, inc, dlt = (small(14700 + 16 * k, NE) for k in range(4))
        posf = small(14800, NT, 2)
        cmp7 = small(14840, OVF, NE)
        w4 = sb("w4", [P, NG])
        w16 = sb("w16", [P, NE])
        e128 = sb("e128", [P, NE])
        j7 = sb("j7", [P, OVF])
        xe = area(0, 4 * D, "p (b n) -> p b n", b=4)
        xeT = area(4096, 2 * KC * P, "p (b c n) -> p b c n", b=2, c=KC)
        ssb = area(6144, 2 * F, "p (b n) -> p b n", b=2)
        hsb = area(6656, 2 * F, "p (b n) -> p b n", b=2)
        hT = area(7168, 2 * FC * P, "p (b c n) -> p b c n", b=2, c=FC)
        ysb = area(7680, 2 * D, "p (b n) -> p b n", b=2)
        gy = area(9728, 4 * D, "p (b k n) -> p b k n", b=2, k=2)

        bank = [ctx.enter_context(nc.psum_tensor(f"bank{i}", [P, 512], fp32)) for i in range(8)]

        xs = nc.dram_tensor("xs", [SLOTS, D], fp32).ap()
        ys = nc.dram_tensor("ys", [SLOTS, D], fp32).ap()
        cd = nc.dram_tensor("cd", [NH, SEQ], fp32).ap()
        xs_t = xs.rearrange("(e p) d -> e p d", p=CAP)
        ys_t = ys.rearrange("(e p) d -> e p d", p=CAP)

        sems = {}

        def S(name):
            if name not in sems:
                sems[name] = ctx.enter_context(nc.semaphore(name))
            return sems[name]

        def chain(eng, name):
            n = [0]

            def link(ins):
                n[0] += 1
                ins.then_inc(S(name), 1)
                eng.wait_ge(S(name), n[0])
            return link

        def slot_in(k):
            return ring[:, k % RING, 0:KC * BLK].rearrange("p (c n) -> p c n", c=KC)

        def slot_down(k):
            return ring[:, k % RING, KC * BLK:SLOT_WORDS].rearrange("p (c n) -> p c n", c=FC)

        def weights_here(eng, k, more=0):
            eng.wait_ge(S(f"w_loaded{k % RING}"), ring_count(k) + more)

        def n_dmas(k):
            return 3 if any(EXP_USE[l] <= k < EXP_USE[l] + NE for l in range(DEPTH)) else 1

        def ring_count(k):
            return 16 * sum(n_dmas(j) for j in range(k % RING, k + 1, RING))

        OV_STEPS = 11
        UNIT = [(hp, n, half) for hp in range(PAIRS) for n in range(NT) for half in range(2)]
        GROUPS = (IN_BLOCKS[0] * NT, 4 * 4 + 2 * NT)

        block = ctx.enter_context(nc.Block())

        @block.sync
        def _(eng):
            eng.dma_start(xres[:, :, :], x[0].rearrange("(t p) d -> p t d", p=P)).then_inc(S("x_in"), 16)

            def load_block(k, src):
                if k >= RING:
                    eng.wait_ge(S("w_used"), k - RING + 1)
                eng.dma_start(slot_in(k), src.rearrange("(c p) n -> p c n", p=P)).then_inc(S(f"w_loaded{k % RING}"), 16)

            def load_expert(s, w, e, sem):
                gu = slot_in(s)
                eng.dma_start(gu[:, :, 0:F], w_gate[w, e].rearrange("(c p) f -> p c f", p=P)).then_inc(sem, 16)
                eng.dma_start(gu[:, :, F:2 * F], w_up[w, e].rearrange("(c p) f -> p c f", p=P)).then_inc(sem, 16)
                eng.dma_start(slot_down(s), w_down[w, e].rearrange("(c p) n -> p c n", p=P)).then_inc(sem, 16)

            for l, (w_in, w_o) in enumerate(((swa_w_in[0], swa_w_o[0]), (fox_w_in[0], fox_w_o[0]))):
                for j in range(IN_BLOCKS[l]):
                    load_block(IN_USE[l] + j, w_in[:, BLK * j:BLK * (j + 1)])
                    if l == 0 and j == 0:
                        eng.dma_start(cs[:, :, :, :], rope.rearrange("(t p) a n -> p t a n", p=P)).then_inc(S("const_in"), 16)
                        eng.dma_start(sink[:, :], swa_sinks[0].partition_broadcast(P)).then_inc(S("const_in"), 16)
                        eng.dma_start(wr[:, :, :], w_router.rearrange("(c p) n -> p c n", p=P)).then_inc(S("const_in"), 16)
                        eng.dma_start(br[:, :], b_router.partition_broadcast(P)).then_inc(S("const_in"), 16)
                        eng.dma_start(bf[:, :], fox_b_f.rearrange("a h -> h a")).then_inc(S("const_in"), 16)
                        eng.dma_start(wf[:, :, :], fox_w_in[0][:, 3 * D:3 * D + NH].rearrange("(c p) n -> p c n", p=P)).then_inc(S("const_in"), 16)
                for j in range(OUT_BLOCKS):
                    load_block(OUT_USE[l] + j, w_o[:, BLK * j:BLK * (j + 1)])
                with eng.Fori(0, NE // RING) as i:
                    for u in range(RING):
                        k = EXP_USE[l] + u
                        eng.wait_ge(S("w_used"), RING * i + (k - RING + 1))
                        load_expert(k, l, RING * i + u, S(f"w_loaded{k % RING}"))
                eng.wait_ge(S(f"routed{l}"), 1)
                n_ovf = eng.value_load(ovf_id[0:1, OVF:OVF + 1], min_val=0, max_val=OVF)
                k = EXP_USE[l] + NE
                with eng.If(n_ovf > 0):
                    eng.wait_ge(S("w_used"), k - RING + 1)
                    with eng.Fori(0, OVF) as j:
                        e = eng.value_load(ovf_id[0:1, bass.ds(j, 1)], min_val=0, max_val=NE - 1)
                        eng.wait_ge(S(f"ov_turn{l}"), OV_STEPS * (j + 1))
                        load_expert(k, l, e, S(f"ov_in{l}"))
                        eng.wait_ge(S(f"ov_turn{l}"), OV_STEPS * (j + 1) + 11)
                        eng.dma_start(ys_t[j + NE], ysb[:, 0, :]).then_inc(S(f"ov_stored{l}"), 16)
            for t in range(NT):
                eng.wait_ge(S(f"x_ready{l}1"), t + 1)
                eng.dma_start(out[0, t * P:(t + 1) * P, :], xres[:, t, :]).then_inc(S("out_done"), 16)
            eng.wait_ge(S("out_done"), 16 * NT)

        @block.gpsimd
        def _(eng):
            link = chain(eng, "pool_step")
            link(eng.memset(ident[:, :], 0.0))
            link(eng.affine_select(out=ident[:, :], in_=ident[:, :], compare_op=ALU.not_equal, fill=1.0,
                                   base=0, pattern=[[-1, P]], channel_multiplier=1))
            link(eng.memset(ones[:, :], 1.0))
            link(eng.affine_select(out=before[:, :], in_=ones[:, :], compare_op=ALU.is_ge, fill=0.0,
                                   base=-1, pattern=[[1, P]], channel_multiplier=-1))
            link(eng.memset(band[:, :, :], 0.0))
            link(eng.memset(causal[:, :], 0.0))
            link(eng.affine_select(out=band[:, 0, :], in_=band[:, 0, :], compare_op=ALU.is_ge, fill=NEG / SCALE,
                                   base=-1, pattern=[[1, P]], channel_multiplier=-1))
            link(eng.affine_select(out=band[:, 1, :], in_=band[:, 1, :], compare_op=ALU.is_ge, fill=NEG / SCALE,
                                   base=0, pattern=[[-1, P]], channel_multiplier=1))
            link(eng.affine_select(out=causal[:, :], in_=causal[:, :], compare_op=ALU.is_ge, fill=NEG / SCALE,
                                   base=0, pattern=[[-1, P]], channel_multiplier=1))
            link(eng.iota(w4[:, :], [[-1, NG]], base=NG, channel_multiplier=0, allow_small_or_imprecise_dtypes=True))
            link(eng.iota(w16[:, :], [[-1, NE]], base=NE, channel_multiplier=0, allow_small_or_imprecise_dtypes=True))
            link(eng.iota(e128[:, :], [[CAP, NE]], base=0, channel_multiplier=0, allow_small_or_imprecise_dtypes=True))
            link(eng.iota(j7[:, :], [[1, OVF]], base=0, channel_multiplier=0, allow_small_or_imprecise_dtypes=True))
            link(eng.memset(mhalf[:, :], -0.5))
            eng.memset(zeros, 0.0).then_inc(S("consts"), 1)
            eng.wait_ge(S("consts"), 1)
            eng.wait_ge(S(f"w_loaded{2}"), 16)
            eng.dma_start(xs.rearrange("(e p) d -> p e d", p=CAP),
                          zeros.unsqueeze(1).to_broadcast([P, NE + OVF, D])).then_inc(S("cleared"), 16)
            eng.dma_start(ys.rearrange("(e p) d -> p e d", p=CAP)[:, NE:NE + OVF, :],
                          zeros.unsqueeze(1).to_broadcast([P, OVF, D])).then_inc(S("cleared"), 16)
            eng.wait_ge(S("cleared"), 32)
            eng.drain().then_inc(S("zeros_free"), 1)

            def load_norm(l, w):
                eng.dma_start(lnp[:, 0, :], ln_gain[l, w].partition_broadcast(P)).then_inc(S("ln_in"), 16)
                eng.dma_start(lnp[:, 1, :], ln_bias[l, w].partition_broadcast(P)).then_inc(S("ln_in"), 16)

            def norm_rstd(l, w, gather=None):
                for t in range(NT):
                    eng.wait_ge(S(f"ln_stats{l}{w}"), t + 1)
                    link(eng.tensor_scalar(veps[:, t:t + 1], mv[:, t, 1:2], LN_EPS, None, ALU.add))
                    eng.tensor_tensor(rstd[:, t:t + 1], veps[:, t:t + 1], mhalf[:, t:t + 1], ALU.pow).then_inc(S(f"rstd{l}{w}"), 1)
                    if gather and t + 2 < NT:
                        gather(t + 2)
                if (l, w) != (DEPTH - 1, 1):
                    eng.wait_ge(S(f"x_ready{l}{w}"), NT)
                    load_norm(*((l, 1) if w == 0 else (l + 1, 0)))

            load_norm(0, 0)
            for l in range(DEPTH):
                if l == 1:
                    eng.wait_ge(S("decay"), 1)
                    eng.dma_start(cd, fz[0:NH, 3, :]).then_inc(S("cd_out"), 16)
                    eng.wait_ge(S("cd_out"), 16)
                    eng.wait_ge(S(f"proj_done{l}"), GROUPS[l])
                    for hp in range(PAIRS):
                        if hp >= 2:
                            eng.wait_ge(S(f"sp_ready{l}"), 2 * NT * (hp - 1))
                        eng.dma_start(cb[:, hp % 2, :, :], cd[2 * hp:2 * hp + 2].partition_broadcast(P)).then_inc(S(f"cb_in{hp % 2}"), 16)
                        eng.wait_ge(S(f"cb_in{hp % 2}"), 16 * (hp // 2 + 1))
                        eng.tensor_tensor(mb[:, hp % 2, :, :].rearrange("p h (n k) -> p (h n) k", k=P),
                                          cb[:, hp % 2, :, :].rearrange("p h (n k) -> p (h n) k", k=P),
                                          causal[:, :].unsqueeze(1).to_broadcast([P, 2 * NT, P]), ALU.add).then_inc(S("mb_ready"), 1)
                norm_rstd(l, 0)
                eng.wait_ge(S(f"routed{l}"), 1)
                for t in range(NT):
                    for k in range(TOPK):
                        eng.indirect_dma_start(xs, bass.IndirectOffsetOnAxis(ap=pos[:, t, k:k + 1], axis=0),
                                               xres[:, t, :], None).then_inc(S(f"scattered{l}"), 16)
                for b in range(2):
                    eng.wait_ge(S(f"y_stored{l}{b}"), 16 * NE // 2)
                n_ovf = eng.value_load(ovf_id[0:1, OVF:OVF + 1], min_val=0, max_val=OVF)
                with eng.If(n_ovf > 0):
                    eng.sem_inc(S(f"ov_turn{l}"), OV_STEPS)
                    with eng.Fori(0, OVF) as j:
                        eng.dma_start(xe[:, 0, :], xs_t[j + NE]).then_inc(S(f"ov_in{l}"), 16)
                        eng.wait_ge(S(f"ov_stored{l}"), 16 * j + 16)
                def gather(t):
                    if t >= 2:
                        eng.wait_ge(S(f"mixed{l}"), t - 1)
                    for k in range(TOPK):
                        eng.indirect_dma_start(gy[:, t % 2, k, :], None, ys,
                                               bass.IndirectOffsetOnAxis(ap=pos[:, t, k:k + 1], axis=0)).then_inc(S(f"gy_in{l}{t % 2}"), 16)
                gather(0)
                gather(1)
                norm_rstd(l, 1, gather)

        @block.tensor
        def _(eng):
            def turn_x(t, a, ready, n_ready):
                eng.wait_ge(S(ready), n_ready)
                if t >= 1:
                    eng.wait_ge(S(f"xt_act{a}"), t)
                    eng.wait_ge(S(f"xt_dve{a}"), t)
                for c in range(KC):
                    mm = eng.transpose(bank[3 + c // 4][:, (c % 4) * P:(c % 4 + 1) * P],
                                       xres[:, t, c * P:(c + 1) * P], ident[:, :])
                mm.then_inc(S(f"xt_done{a}"), 1)

            eng.wait_ge(S("consts"), 1)
            for t in range(NT):
                turn_x(t, "in", "x_in", 16)
            for l in range(DEPTH):
                a = "in" if l == 0 else "01"
                eng.wait_ge(S(f"xt_act{a}"), NT)
                eng.wait_ge(S(f"xt_dve{a}"), NT)

                def project(k, lhs, rhs, use, last):
                    if k >= 2:
                        eng.wait_ge(S(f"proj_free{l}{k % 2}"), k // 2)
                    weights_here(eng, use)
                    for c in range(KC):
                        mm = eng.matmul(bank[k % 2][:, :], lhs(c), rhs(c), start=(c == 0), stop=(c == KC - 1))
                    mm.then_inc(S(f"proj_done{l}"), 1)

                if l == 0:
                    def turn_heads(k):
                        eng.wait_ge(S("roped"), k + 1)
                        if k >= 2:
                            eng.wait_ge(S("qkT_free"), k - 1)
                        for i in range(4):
                            mm = eng.transpose(bank[5 + k % 2][:, i * P:(i + 1) * P], tok[:, k % 2, i * P:(i + 1) * P], ident[:, :])
                        mm.then_inc(S("qkT_done"), 1)

                    for j in range(IN_BLOCKS[0]):
                        for t in range(NT):
                            k = NT * j + t
                            w = slot_in(j)
                            project(k, lambda c: xT[:, c, t * P:(t + 1) * P], lambda c: w[:, c, :], j, t == NT - 1)
                            if k >= 1:
                                turn_heads(k - 1)
                        eng.drain().then_inc(S("w_used"), 1)
                    turn_heads(GROUPS[0] - 1)
                    eng.wait_ge(S("qkT_free"), GROUPS[0])
                else:
                    eng.wait_ge(S("const_in"), 96)
                    for c in range(KC):
                        mm = eng.matmul(bank[7][0:NH, :], wf[:, c, :], xT[:, c, :], start=(c == 0), stop=(c == KC - 1))
                    mm.then_inc(S("forget"), 1)
                    for j in range(IN_BLOCKS[1]):
                        w = slot_in(IN_USE[1] + j)
                        for t in range(4):
                            k = 4 * j + t
                            if j < 4:
                                project(k, lambda c: w[:, c, t * P:(t + 1) * P], lambda c: xT[:, c, :], IN_USE[1] + j, t == 3)
                            else:
                                project(k, lambda c: xT[:, c, t * P:(t + 1) * P], lambda c: w[:, c, :], IN_USE[1] + j, t == 3)
                        eng.drain().then_inc(S("w_used"), 1)
                    for b in range(2):
                        eng.wait_ge(S(f"proj_free{l}{b}"), GROUPS[1] // 2)

                def keys(n):
                    return (max(n - 1, 0), n + 1) if l == 0 else (0, n + 1)

                def scores(u):
                    hp, n, half = UNIT[u]
                    k0, k1 = keys(n)
                    if u >= 3:
                        eng.wait_ge(S(f"sp_ready{l}"), u - 2)
                    r = slice(HD * half, HD * half + HD)
                    kp = (2 * hp + half) // (NH // NKV) if l == 0 else hp
                    eng.matmul(bank[u % 3][:, 0:(k1 - k0) * P], QT[r, hp, n * P:(n + 1) * P], KT[r, kp, k0 * P:k1 * P],
                               start=True, stop=True).then_inc(S(f"s_done{l}"), 1)

                def turn_probs(u):
                    hp, n, half = UNIT[u]
                    k0, k1 = keys(n)
                    eng.wait_ge(S(f"p_ready{l}"), u + 1)
                    if u >= 2:
                        eng.wait_ge(S(f"pT_ready{l}{half}"), u // 2)
                    for i in range(k1 - k0):
                        mm = eng.transpose(bank[3 + u % 2][:, i * P:(i + 1) * P], sp[:, u % 3, i * P:(i + 1) * P], ident[:, :])
                    mm.then_inc(S(f"pT_done{l}"), 1)

                def mix(u):
                    hp, n, half = UNIT[u]
                    k0, k1 = keys(n)
                    k = u // 2
                    eng.wait_ge(S(f"pT_ready{l}{half}"), k + 1)
                    if k >= 2 and half == 0:
                        eng.wait_ge(S(f"heads_ready{l}"), k - 1)
                    v = HD * ((2 * hp + half) // (NH // NKV) if l == 0 else 2 * hp + half)
                    for i in range(k1 - k0):
                        mm = eng.matmul(bank[5 + k % 2][:, HD * half:HD * half + HD], pT[:, u % 2, i * P:(i + 1) * P],
                                        V[:, k0 + i, v:v + HD], start=(i == 0), stop=(i == k1 - k0 - 1))
                    mm.then_inc(S(f"pv_done{l}"), 1)

                def turn_out(k):
                    eng.wait_ge(S(f"heads_ready{l}"), k + 1)
                    if k >= 1:
                        eng.wait_ge(S(f"aT_ready{l}"), k)
                    eng.transpose(bank[7][:, 0:P], heads[:, k % 2, :], ident[:, :]).then_inc(S(f"aT_done{l}"), 1)

                scores(0)
                scores(1)
                for u in range(UNITS):
                    if u >= 3 and u % 2 == 1:
                        turn_out((u - 3) // 2)
                    if u + 2 < UNITS:
                        scores(u + 2)
                    turn_probs(u)
                    if u >= 1:
                        mix(u - 1)
                mix(UNITS - 1)
                turn_out(UNITS // 2 - 1)

                eng.wait_ge(S(f"aT_ready{l}"), UNITS // 2)
                for t in range(NT):
                    for b in range(OUT_BLOCKS):
                        g = OUT_BLOCKS * t + b
                        if g >= 2:
                            eng.wait_ge(S(f"res_done{l}"), g - 1)
                        weights_here(eng, OUT_USE[l] + b)
                        w = slot_in(OUT_USE[l] + b)
                        for c in range(KC):
                            mm = eng.matmul(bank[b][:, :], QT[:, c, t * P:(t + 1) * P], w[:, c, :], start=(c == 0), stop=(c == KC - 1))
                        mm.then_inc(S(f"wo_done{l}"), 1)
                    if t >= 1:
                        turn_x(t - 1, f"{l}0", f"x_ready{l}0", t)
                eng.drain().then_inc(S("w_used"), OUT_BLOCKS)
                turn_x(NT - 1, f"{l}0", f"x_ready{l}0", NT)

                for t in range(NT):
                    eng.wait_ge(S(f"xt_act{l}0"), t + 1)
                    eng.wait_ge(S(f"xt_dve{l}0"), t + 1)
                    if t == 0:
                        eng.wait_ge(S("const_in"), 96)
                    for c in range(KC):
                        mm = eng.matmul(bank[7][:, t * NE:(t + 1) * NE], xT[:, c, t * P:(t + 1) * P], wr[:, c, :],
                                        start=(c == 0), stop=(c == KC - 1))
                mm.then_inc(S(f"logits{l}"), 1)
                eng.wait_ge(S(f"assigned{l}"), 1)
                asn_f = asn.rearrange("p t e -> p (t e)")
                eng.matmul(bank[2][:, 0:NT * NE], before[:, :], asn_f, start=True, stop=False)
                for m in range(NT - 1):
                    for t in range(m + 1, NT):
                        eng.matmul(bank[2][:, t * NE:(t + 1) * NE], ones[:, :], asn[:, m, :], start=False,
                                   stop=(m == NT - 2))
                for m in range(NT):
                    mm = eng.matmul(bank[6][:, 0:NE], ones[:, :], asn[:, m, :], start=(m == 0), stop=(m == NT - 1))
                mm.then_inc(S(f"ranked{l}"), 1)

                def turn_rows(b):
                    for c in range(KC):
                        mm = eng.transpose(bank[c // 4][:, (c % 4) * P:(c % 4 + 1) * P], xe[:, b, c * P:(c + 1) * P], ident[:, :])
                    return mm

                def gate_up(b, use):
                    w = slot_in(use)
                    for c in range(KC):
                        mm = eng.matmul(bank[2 + b][:, :], xeT[:, b, c, :], w[:, c, :], start=(c == 0), stop=(c == KC - 1))
                    return mm

                def turn_h(b):
                    for c in range(FC):
                        mm = eng.transpose(bank[4][:, c * P:(c + 1) * P], hsb[:, b, c * P:(c + 1) * P], ident[:, :])
                    return mm

                def down(b, use):
                    w = slot_down(use)
                    for half in range(2):
                        for c in range(FC):
                            mm = eng.matmul(bank[5 + half][:, :], hT[:, b, c, :], w[:, c, half * BLK:(half + 1) * BLK],
                                            start=(c == 0), stop=(c == FC - 1))
                    return mm

                def step(i, u, first=False, last=False):
                    use = EXP_USE[l] + u
                    e = 4 * i + u
                    eng.wait_ge(S(f"xeT_act{l}"), e + 1)
                    eng.wait_ge(S(f"xeT_dve{l}"), e + 1)
                    eng.wait_ge(S(f"w_loaded{use % RING}"), 48 * i + ring_count(use))
                    gate_up(u % 2, use).then_inc(S(f"gu_done{l}"), 1)
                    if not first:
                        eng.wait_ge(S(f"h_ready{l}"), e)
                        turn_h((u - 1) % 2).then_inc(S(f"hT_done{l}"), 1)
                    if not last:
                        eng.wait_ge(S(f"xe_in{l}{(u + 1) % 4}"), 16 * i + 16 * ((u + 1) // 4) + 16)
                        turn_rows((u + 1) % 4).then_inc(S(f"xeT_done{l}"), 1)
                    if not first:
                        down_of(e - 1, (u - 1) % 2, use - 1, u > 1 or not isinstance(i, int) or i > 0)

                def down_of(e, b, use, reused):
                    eng.wait_ge(S(f"hT_ready{l}"), e + 1)
                    if reused:
                        eng.wait_ge(S(f"y_act{l}"), e)
                        eng.wait_ge(S(f"y_dve{l}"), e)
                    down(b, use).then_inc(S(f"y_done{l}"), 1)
                    eng.drain().then_inc(S("w_used"), 1)

                eng.wait_ge(S(f"xe_in{l}0"), 16)
                turn_rows(0).then_inc(S(f"xeT_done{l}"), 1)
                step(0, 0, first=True)
                step(0, 1)
                with eng.Fori(0, NE // 4 - 1) as i:
                    for u in range(2, 6):
                        step(i, u)
                for u in range(2, 4):
                    step(NE // 4 - 1, u, last=(u == 3))
                eng.wait_ge(S(f"h_ready{l}"), NE)
                turn_h(1).then_inc(S(f"hT_done{l}"), 1)
                down_of(NE - 1, 1, EXP_USE[l] + NE - 1, True)
                n_ovf = eng.value_load(ovf_id[0:1, OVF:OVF + 1], min_val=0, max_val=OVF)
                with eng.If(n_ovf > 0):
                    eng.wait_ge(S(f"y_act{l}"), NE)
                    eng.wait_ge(S(f"y_dve{l}"), NE)
                    with eng.Fori(0, OVF) as j:
                        eng.wait_ge(S(f"ov_in{l}"), 64 * j + 64)
                        turn_rows(0).then_inc(S(f"ov_turn{l}"), 1)
                        eng.wait_ge(S(f"ov_turn{l}"), OV_STEPS * (j + 1) + 3)
                        gate_up(0, EXP_USE[l] + NE).then_inc(S(f"ov_turn{l}"), 1)
                        eng.wait_ge(S(f"ov_turn{l}"), OV_STEPS * (j + 1) + 6)
                        turn_h(0).then_inc(S(f"ov_turn{l}"), 1)
                        eng.wait_ge(S(f"ov_turn{l}"), OV_STEPS * (j + 1) + 8)
                        down(0, EXP_USE[l] + NE).then_inc(S(f"ov_turn{l}"), 1)
                if l + 1 < DEPTH:
                    for t in range(NT):
                        turn_x(t, f"{l}1", f"x_ready{l}1", t + 1)

        @block.scalar
        def _(eng):
            def evac_x(a):
                for t in range(NT):
                    eng.wait_ge(S(f"xt_done{a}"), t + 1)
                    eng.copy(xT[:, 0:4, t * P:(t + 1) * P], bank[3][:, :].rearrange("p (c n) -> p c n", c=4)).then_inc(S(f"xt_act{a}"), 1)

            evac_x("in")
            for l in range(DEPTH):
                if l == 0:
                    for k in range(GROUPS[0]):
                        eng.wait_ge(S("proj_done0"), k + 1)
                        if k >= 2:
                            eng.wait_ge(S("qkT_done"), k - 1)
                        j, t = k // NT, k % NT
                        b = bank[k % 2]
                        if j < 2:
                            cp = eng.copy(tok[:, k % 2, :], b[:, :])
                        else:
                            if t == 2:
                                eng.wait_ge(S("zeros_free"), 1)
                            eng.copy(V[:, t, 0:F], b[:, F:2 * F])
                            cp = eng.copy(tok[:, k % 2, :].rearrange("p (h a d) -> p h a d", a=2, d=HD)[:, :, 0, :],
                                          b[:, 0:F].rearrange("p (h d) -> p h d", d=HD))
                        cp.then_inc(S(f"proj_free0{k % 2}"), 1)
                else:
                    eng.wait_ge(S("fz_abs"), 1)
                    eng.activation(fz[0:NH, 1, :], fz[0:NH, 1, :], ACT.Exp, scale=-1.0).then_inc(S("act_step"), 1)
                    eng.wait_ge(S("act_step"), 1)
                    eng.activation(fz[0:NH, 1, :], fz[0:NH, 1, :], ACT.Ln, bias=1.0).then_inc(S("fz_ln"), 1)
                    for k in range(0, GROUPS[1], 2):
                        eng.wait_ge(S("proj_done1"), k + 1)
                        j, t = k // 4, k % 4
                        dst = QT[:, 4 * j + t, :] if j < 2 else KT[:, 4 * (j - 2) + t, :] if j < 4 else V[:, t, (j - 4) * BLK:(j - 3) * BLK]
                        eng.copy(dst, bank[0][:, :]).then_inc(S("proj_free10"), 1)

                def expo(u):
                    hp, n, half = UNIT[u]
                    nk = P * (min(n, 1) + 1) + 1 if l == 0 else P * (n + 1)
                    eng.wait_ge(S(f"sp_ready{l}"), u + 1)
                    eng.activation(sp[:, u % 3, 0:nk], sp[:, u % 3, 0:nk], ACT.Exp, bias=nmax[:, u % 4:u % 4 + 1], scale=-1.0,
                                   accum_out=rsum[:, (u // 2) % 4, half:half + 1]).then_inc(S(f"p_ready{l}"), 1)

                expo(0)
                for u in range(UNITS):
                    if u + 1 < UNITS:
                        expo(u + 1)
                    hp, n, half = UNIT[u]
                    if half == 0:
                        nk = P * (min(n, 1) + 1) if l == 0 else P * (n + 1)
                        eng.wait_ge(S(f"pT_done{l}"), u + 1)
                        if u >= 2:
                            eng.wait_ge(S(f"pv_done{l}"), u - 1)
                        eng.copy(pT[:, u % 2, 0:nk], bank[3 + u % 2][:, 0:nk]).then_inc(S(f"pT_ready{l}0"), 1)

                evac_x(f"{l}0")
                eng.wait_ge(S(f"shifted{l}"), 1)
                eng.activation(pr, lg, ACT.Exp).then_inc(S(f"expd{l}"), 1)

                def load_rows(e, b):
                    eng.dma_start(xe[:, b, :], xs_t[e]).then_inc(S(f"xe_in{l}{b}"), 16)

                def store_rows(e, b):
                    eng.wait_ge(S(f"y_dve{l}"), e + 1)
                    eng.wait_ge(S(f"y_act{l}"), e + 1)
                    eng.dma_start(ys_t[e], ysb[:, b, :]).then_inc(S(f"y_stored{l}{b}"), 16)

                def evac_rows(e, b):
                    eng.wait_ge(S(f"xeT_done{l}"), e + 1)
                    eng.copy(xeT[:, b, 0:4, :], bank[0][:, :].rearrange("p (c n) -> p c n", c=4)).then_inc(S(f"xeT_act{l}"), 1)

                def silu(e, b):
                    eng.wait_ge(S(f"gu_done{l}"), e + 1)
                    eng.activation(ssb[:, b, :], bank[2 + b][:, 0:F], ACT.Silu).then_inc(S(f"silu{l}"), 1)

                def evac_y(e, b, stored):
                    eng.wait_ge(S(f"y_done{l}"), e + 1)
                    if stored is not None:
                        eng.wait_ge(S(f"y_stored{l}{b}"), stored)
                    eng.copy(ysb[:, b, 0:BLK], bank[5][:, :]).then_inc(S(f"y_act{l}"), 1)

                def step(i, u, first=False, last=False):
                    e = 4 * i + u
                    silu(e, u % 2)
                    if not last:
                        evac_rows(e + 1, (u + 1) % 2)
                        if not isinstance(i, int) or e + 5 < NE:
                            load_rows(e + 5, (u + 1) % 4)
                    if not first:
                        started = not isinstance(i, int) or 4 * i + u - 1 >= 2
                        evac_y(e - 1, (u - 1) % 2, 32 * i + 16 * ((u - 1) // 2) if started else None)
                        store_rows(e - 1, (u - 1) % 2)

                eng.wait_ge(S(f"scattered{l}"), 16 * NT * TOPK)
                for b in range(4):
                    load_rows(b, b)
                evac_rows(0, 0)
                load_rows(4, 0)
                for u in range(3):
                    step(0, u, first=(u == 0))
                with eng.Fori(0, NE // 4 - 2) as i:
                    for u in range(3, 7):
                        step(i, u)
                for u in range(3, 8):
                    step(NE // 4 - 2, u, last=(u == 7))
                evac_y(NE - 1, 1, 16 * ((NE - 1) // 2))
                store_rows(NE - 1, 1)
                n_ovf = eng.value_load(ovf_id[0:1, OVF:OVF + 1], min_val=0, max_val=OVF)
                with eng.If(n_ovf > 0):
                    eng.wait_ge(S(f"y_stored{l}0"), 16 * NE // 2)
                    with eng.Fori(0, OVF) as j:
                        eng.wait_ge(S(f"ov_turn{l}"), OV_STEPS * (j + 1) + 1)
                        eng.copy(xeT[:, 0, 0:4, :], bank[0][:, :].rearrange("p (c n) -> p c n", c=4)).then_inc(S(f"ov_turn{l}"), 1)
                        eng.wait_ge(S(f"ov_turn{l}"), OV_STEPS * (j + 1) + 4)
                        eng.activation(ssb[:, 0, :], bank[2][:, 0:F], ACT.Silu).then_inc(S(f"ov_turn{l}"), 1)
                        eng.wait_ge(S(f"ov_turn{l}"), OV_STEPS * (j + 1) + 9)
                        eng.copy(ysb[:, 0, 0:BLK], bank[5][:, :]).then_inc(S(f"ov_turn{l}"), 1)
                for t in range(NT):
                    eng.wait_ge(S(f"gy_in{l}{t % 2}"), 32 * (t // 2 + 1))
                    eng.activation(gy[:, t % 2, 0, :], gy[:, t % 2, 0, :], ACT.Copy, scale=gates[:, t, 0:1]).then_inc(S(f"gated{l}"), 1)
                if l + 1 < DEPTH:
                    evac_x(f"{l}1")

        @block.vector
        def _(eng):
            link = chain(eng, "dve_step")

            def evac_x_tile(a, t):
                eng.wait_ge(S(f"xt_done{a}"), t + 1)
                eng.tensor_copy(xT[:, 4:8, t * P:(t + 1) * P], bank[4][:, :].rearrange("p (c n) -> p c n", c=4)).then_inc(S(f"xt_dve{a}"), 1)

            norms = [0]

            def norm(l, w, t):
                v = xres[:, t, :]
                if t == 0:
                    norms[0] += 1
                    eng.wait_ge(S("ln_in"), 32 * norms[0])
                eng.bn_stats(stats[:, t, 0, :], xres[:, t, 0:BLK])
                link(eng.bn_stats(stats[:, t, 1, :], xres[:, t, BLK:D]))
                eng.bn_aggr(mv[:, t, :], stats[:, t, :, :].rearrange("p a b -> p (a b)")).then_inc(S(f"ln_stats{l}{w}"), 1)
                eng.wait_ge(S(f"ln_stats{l}{w}"), t + 1)
                link(eng.scalar_tensor_tensor(v, v, mv[:, t, 0:1], lnp[:, 0, :], ALU.subtract, ALU.mult))
                eng.wait_ge(S(f"rstd{l}{w}"), t + 1)
                eng.scalar_tensor_tensor(v, v, rstd[:, t:t + 1], lnp[:, 1, :], ALU.mult, ALU.add).then_inc(S(f"x_ready{l}{w}"), 1)

            for t in range(NT):
                evac_x_tile("in", t)
            eng.wait_ge(S("const_in"), 96)
            link(eng.tensor_scalar(sink[:, :], sink[:, :], -1.0, None, ALU.mult))
            for l in range(DEPTH):
                if l == 0:
                    def evac_heads(k):
                        eng.wait_ge(S("qkT_done"), k + 1)
                        j, t = k // NT, k % NT
                        dst = QT[:, 4 * j:4 * j + 4, :] if j < 2 else KT[:, 0:4, :]
                        eng.tensor_copy(dst[:, :, t * P:(t + 1) * P],
                                        bank[5 + k % 2][:, :].rearrange("p (h n) -> p h n", h=4)).then_inc(S("qkT_free"), 1)

                    for k in range(GROUPS[0]):
                        j, t = k // NT, k % NT
                        eng.wait_ge(S(f"proj_free0{k % 2}"), k // 2 + 1)
                        if j < 2:
                            nh, hv = 8, tok[:, k % 2, :].rearrange("p (h d) -> p h d", d=HD)
                        else:
                            kd = tok[:, k % 2, :].rearrange("p (h a d) -> p h a d", a=2, d=HD)
                            nh, hv = 4, kd[:, :, 0, :]
                        r = hv[:, :, 0:ROT]
                        if k >= 1:
                            eng.wait_ge(S("roped"), k)
                        tc = rtmp[:, 0, 0:nh * ROT].rearrange("p (h d) -> p h d", h=nh)
                        ts = rtmp[:, 1, 0:nh * ROT].rearrange("p (h d) -> p h d", h=nh)
                        eng.tensor_tensor(tc, r, cs[:, t, 0, :].unsqueeze(1).to_broadcast([P, nh, ROT]), ALU.mult)
                        link(eng.tensor_tensor(ts, r, cs[:, t, 1, :].unsqueeze(1).to_broadcast([P, nh, ROT]), ALU.mult))
                        h = ROT // 2
                        rot = eng.tensor_tensor(hv[:, :, 0:h], tc[:, :, 0:h], ts[:, :, h:ROT], ALU.subtract)
                        if j < 2:
                            eng.tensor_tensor(hv[:, :, h:ROT], tc[:, :, h:ROT], ts[:, :, 0:h], ALU.add).then_inc(S("roped"), 1)
                        else:
                            link(eng.tensor_tensor(hv[:, :, h:ROT], tc[:, :, h:ROT], ts[:, :, 0:h], ALU.add))
                            eng.tensor_copy(kd[:, :, 1, :], kd[:, :, 0, :]).then_inc(S("roped"), 1)
                        if k >= 1:
                            evac_heads(k - 1)
                    evac_heads(GROUPS[0] - 1)
                else:
                    eng.wait_ge(S("forget"), 1)
                    z, az, ls, c = (fz[0:NH, k, :] for k in range(4))
                    link(eng.tensor_scalar(z, bank[7][0:NH, :], bf[:, 0:1], None, ALU.add))
                    link(eng.tensor_scalar(az, z, -1.0, None, ALU.mult))
                    eng.tensor_tensor(az, az, z, ALU.max).then_inc(S("fz_abs"), 1)
                    link(eng.tensor_scalar(z, z, 0.0, None, ALU.min))
                    eng.wait_ge(S("fz_ln"), 1)
                    link(eng.tensor_tensor(ls, z, az, ALU.subtract))
                    link(eng.memset(z, 0.0))
                    link(eng.tensor_tensor_scan(c, ls, z, 0.0, ALU.add, ALU.add))
                    eng.tensor_scalar(c, c, -1.0 / SCALE, None, ALU.mult).then_inc(S("decay"), 1)
                    for k in range(1, GROUPS[1], 2):
                        eng.wait_ge(S("proj_done1"), k + 1)
                        j, t = k // 4, k % 4
                        dst = QT[:, 4 * j + t, :] if j < 2 else KT[:, 4 * (j - 2) + t, :] if j < 4 else V[:, t, (j - 4) * BLK:(j - 3) * BLK]
                        eng.tensor_copy(dst, bank[1][:, :]).then_inc(S("proj_free11"), 1)
                    eng.wait_ge(S("cd_out"), 16)

                def mask_and_max(u):
                    hp, n, half = UNIT[u]
                    h = 2 * hp + half
                    eng.wait_ge(S(f"s_done{l}"), u + 1)
                    if u >= 3:
                        eng.wait_ge(S(f"pT_done{l}"), u - 2)
                    s, o, m = bank[u % 3], sp[:, u % 3, :], nmax[:, u % 4:u % 4 + 1]
                    if l == 0:
                        nk = P * (min(n, 1) + 1)
                        bias = band[:, :, :].rearrange("p a k -> p (a k)")[:, 2 * P - nk:2 * P]
                        eng.tensor_copy(o[:, nk:nk + 1], sink[:, h:h + 1])
                        eng.tensor_tensor_reduce(out=o[:, 0:nk], in0=s[:, 0:nk], in1=bias, scale=-SCALE,
                                                 scalar=sink[:, h:h + 1], op0=ALU.add, op1=ALU.min,
                                                 accum_out=m).then_inc(S("sp_ready0"), 1)
                    else:
                        if n == 0 and half == 0:
                            eng.wait_ge(S("mb_ready"), hp + 1)
                            eng.wait_ge(S(f"cb_in{hp % 2}"), 16 * (hp // 2 + 1))
                        d0 = n * P
                        first = -NEG
                        if n:
                            m1 = nmax1[:, u % 4:u % 4 + 1]
                            link(eng.tensor_tensor_reduce(out=o[:, 0:d0], in0=s[:, 0:d0], in1=cb[:, hp % 2, half, 0:d0],
                                                          scale=-SCALE, scalar=-NEG, op0=ALU.add, op1=ALU.min, accum_out=m1))
                            first = m1
                        eng.tensor_tensor_reduce(out=o[:, d0:d0 + P], in0=s[:, d0:d0 + P], in1=mb[:, hp % 2, half, d0:d0 + P],
                                                 scale=-SCALE, scalar=first, op0=ALU.add, op1=ALU.min,
                                                 accum_out=m).then_inc(S("sp_ready1"), 1)

                def evac_out(k):
                    hp, n, _ = UNIT[2 * k]
                    eng.wait_ge(S(f"aT_done{l}"), k + 1)
                    eng.tensor_copy(QT[:, hp, n * P:(n + 1) * P], bank[7][:, 0:P]).then_inc(S(f"aT_ready{l}"), 1)

                mask_and_max(0)
                for u in range(UNITS):
                    if u >= 3 and u % 2 == 1:
                        evac_out((u - 3) // 2)
                    if u + 1 < UNITS:
                        mask_and_max(u + 1)
                    hp, n, half = UNIT[u]
                    if half == 1:
                        nk = P * (min(n, 1) + 1) if l == 0 else P * (n + 1)
                        eng.wait_ge(S(f"pT_done{l}"), u + 1)
                        if u >= 2:
                            eng.wait_ge(S(f"pv_done{l}"), u - 1)
                        eng.tensor_copy(pT[:, u % 2, 0:nk], bank[3 + u % 2][:, 0:nk]).then_inc(S(f"pT_ready{l}1"), 1)
                    if u >= 2 and u % 2 == 0 or u == UNITS - 1:
                        for k in ([u // 2 - 1] if u % 2 == 0 else [u // 2]):
                            eng.wait_ge(S(f"pv_done{l}"), 2 * k + 2)
                            if k >= 2:
                                eng.wait_ge(S(f"aT_done{l}"), k - 1)
                            link(eng.reciprocal(rinv[:, k % 4, :], rsum[:, k % 4, :]))
                            eng.tensor_tensor(heads[:, k % 2, :].rearrange("p (h d) -> p h d", h=2),
                                              bank[5 + k % 2][:, 0:P].rearrange("p (h d) -> p h d", h=2),
                                              rinv[:, k % 4, :].unsqueeze(2).to_broadcast([P, 2, HD]), ALU.mult).then_inc(S(f"heads_ready{l}"), 1)
                evac_out(UNITS // 2 - 1)

                for t in range(NT):
                    for b in range(OUT_BLOCKS):
                        eng.wait_ge(S(f"wo_done{l}"), OUT_BLOCKS * t + b + 1)
                        v = xres[:, t, b * BLK:(b + 1) * BLK]
                        ins = eng.scalar_tensor_tensor(v, v, ALPHA, bank[b][:, :], ALU.mult, ALU.add)
                        ins.then_inc(S(f"res_done{l}"), 1)
                    eng.wait_ge(S(f"res_done{l}"), OUT_BLOCKS * (t + 1))
                    norm(l, 0, t)
                    if t >= 1:
                        evac_x_tile(f"{l}0", t - 1)
                evac_x_tile(f"{l}0", NT - 1)

                def over(a, n):
                    return a.unsqueeze(2).to_broadcast([P, a.shape[1], n])

                def tiles(a):
                    return a.unsqueeze(1).to_broadcast([P, NT, a.shape[1]])

                mx, sm, rs, gm, kb, v1, k1, v2, k2 = (red[:, k, :] for k in range(9))
                eng.wait_ge(S(f"logits{l}"), 1)
                lps = bank[7][:, 0:NT * NE].rearrange("p (t e) -> p t e", t=NT)
                link(eng.tensor_tensor(lg, lps, tiles(br[:, :]), ALU.add))
                link(eng.tensor_reduce(mx, lg, X, ALU.max))
                eng.tensor_tensor(lg, lg, over(mx, NE), ALU.subtract).then_inc(S(f"shifted{l}"), 1)
                eng.wait_ge(S(f"expd{l}"), 1)
                link(eng.tensor_reduce(sm, pr, X, ALU.add))
                link(eng.reciprocal(rs, sm))
                link(eng.tensor_tensor(pr, pr, over(rs, NE), ALU.mult))
                eng.tensor_tensor(pair[:, :, :, 0:3], prg[:, :, :, 0:3], prg[:, :, :, 1:4], ALU.add)
                eng.tensor_tensor(pair[:, :, :, 3:5], prg[:, :, :, 0:2], prg[:, :, :, 2:4], ALU.add)
                link(eng.tensor_tensor(pair[:, :, :, 5:6], prg[:, :, :, 0:1], prg[:, :, :, 3:4], ALU.add))
                link(eng.tensor_reduce(gs, pair, X, ALU.max))
                link(eng.tensor_reduce(gm, gs, X, ALU.max))
                link(eng.tensor_tensor(gk, gs, over(gm, NG), ALU.is_equal))
                link(eng.tensor_tensor(gk, gk, tiles(w4[:, :]), ALU.mult))
                link(eng.tensor_reduce(kb, gk, X, ALU.max))
                link(eng.tensor_tensor(gk, gk, over(kb, NG), ALU.is_equal))
                link(eng.tensor_scalar(gs, gk, -1.0, None, ALU.add))
                mskg = msk.rearrange("p t (g e) -> p t g e", g=NG)
                link(eng.tensor_tensor(mskg, prg, gk.unsqueeze(3).to_broadcast([P, NT, NG, EPG]), ALU.mult))
                link(eng.tensor_tensor(mskg, mskg, gs.unsqueeze(3).to_broadcast([P, NT, NG, EPG]), ALU.add))
                for v, kk, oh in ((v1, k1, oh1), (v2, k2, oh2)):
                    link(eng.tensor_reduce(v, msk, X, ALU.max))
                    link(eng.tensor_tensor(tmp, msk, over(v, NE), ALU.is_equal))
                    link(eng.tensor_tensor(tmp, tmp, tiles(w16[:, :]), ALU.mult))
                    link(eng.tensor_reduce(kk, tmp, X, ALU.max))
                    link(eng.tensor_tensor(oh, tmp, over(kk, NE), ALU.is_equal))
                    if oh is oh1:
                        link(eng.tensor_scalar(tmp, oh1, -4.0, None, ALU.mult))
                        link(eng.tensor_tensor(msk, msk, tmp, ALU.add))
                eng.tensor_tensor(asn, oh1, oh2, ALU.add).then_inc(S(f"assigned{l}"), 1)
                link(eng.tensor_tensor(sm, v1, v2, ALU.add))
                link(eng.reciprocal(rs, sm))
                eng.tensor_tensor(gates[:, :, 0], v1, rs, ALU.mult)
                link(eng.tensor_tensor(gates[:, :, 1], v2, rs, ALU.mult))
                eng.wait_ge(S(f"ranked{l}"), 1)
                link(eng.tensor_copy(cnt, bank[6][:, 0:NE]))
                link(eng.tensor_scalar(ext, cnt, float(CAP), None, ALU.is_gt))
                for m in range(2, NT):
                    link(eng.scalar_tensor_tensor(ext, cnt, float(m * CAP), ext, ALU.is_gt, ALU.add))
                link(eng.memset(dlt, 0.0))
                link(eng.tensor_tensor_scan(inc, ext, dlt, 0.0, ALU.add, ALU.add))
                link(eng.tensor_tensor(dlt, inc, ext, ALU.subtract))
                link(eng.tensor_scalar(dlt, dlt, float(CAP), float(CAP * (NE - 1)), ALU.mult, ALU.add))
                link(eng.tensor_tensor(dlt, dlt, e128[:, :], ALU.subtract))
                rk = bank[2][:, 0:NT * NE].rearrange("p (t e) -> p t e", t=NT)
                link(eng.tensor_copy(tmp, rk))
                link(eng.tensor_scalar(slot, tmp, float(CAP), None, ALU.is_ge))
                link(eng.tensor_tensor(slot, slot, tiles(dlt), ALU.mult))
                link(eng.tensor_tensor(slot, slot, tmp, ALU.add))
                link(eng.tensor_tensor(slot, slot, tiles(e128[:, :]), ALU.add))
                link(eng.tensor_tensor(oh1, oh1, slot, ALU.mult))
                link(eng.tensor_tensor(oh2, oh2, slot, ALU.mult))
                link(eng.tensor_reduce(posf[:, :, 0], oh1, X, ALU.add))
                link(eng.tensor_reduce(posf[:, :, 1], oh2, X, ALU.add))
                link(eng.tensor_copy(pos[:, :, :], posf))
                row = cmp7[0:1]
                link(eng.tensor_tensor(row, inc[0:1].unsqueeze(1).to_broadcast([1, OVF, NE]),
                                       j7[0:1, :].unsqueeze(2).to_broadcast([1, OVF, NE]), ALU.is_le))
                link(eng.tensor_reduce(red[0:1, 9:11, :].rearrange("p a b -> p (a b)")[:, 0:OVF], row, X, ALU.add))
                ids = red[0:1, 9:11, :].rearrange("p a b -> p (a b)")
                link(eng.tensor_scalar(ids[:, 0:OVF], ids[:, 0:OVF], float(NE - 1), None, ALU.min))
                link(eng.tensor_copy(ids[:, OVF:OVF + 1], inc[0:1, NE - 1:NE]))
                eng.tensor_copy(ovf_id[0:1, :], ids).then_inc(S(f"routed{l}"), 1)
                eng.wait_ge(S(f"routed{l}"), 1)

                def evac_rows(e, b):
                    eng.wait_ge(S(f"xeT_done{l}"), e + 1)
                    eng.tensor_copy(xeT[:, b, 4:8, :], bank[1][:, :].rearrange("p (c n) -> p c n", c=4)).then_inc(S(f"xeT_dve{l}"), 1)

                def evac_hT(e, b):
                    eng.wait_ge(S(f"hT_done{l}"), e + 1)
                    eng.tensor_copy(hT[:, b, :, :], bank[4][:, 0:F].rearrange("p (c n) -> p c n", c=FC)).then_inc(S(f"hT_ready{l}"), 1)

                def times_up(e, b):
                    eng.wait_ge(S(f"silu{l}"), e + 1)
                    eng.tensor_tensor(hsb[:, b, :], ssb[:, b, :], bank[2 + b][:, F:2 * F], ALU.mult).then_inc(S(f"h_ready{l}"), 1)

                def evac_y(e, b, stored):
                    eng.wait_ge(S(f"y_done{l}"), e + 1)
                    if stored is not None:
                        eng.wait_ge(S(f"y_stored{l}{b}"), stored)
                    eng.tensor_copy(ysb[:, b, BLK:D], bank[6][:, :]).then_inc(S(f"y_dve{l}"), 1)

                def step(i, u, first=False, last=False):
                    e = 4 * i + u
                    times_up(e, u % 2)
                    if not first:
                        evac_hT(e - 1, (u - 1) % 2)
                    if not last:
                        evac_rows(e + 1, (u + 1) % 2)
                    if not first:
                        started = not isinstance(i, int) or 4 * i + u - 1 >= 2
                        evac_y(e - 1, (u - 1) % 2, 32 * i + 16 * ((u - 1) // 2) if started else None)

                evac_rows(0, 0)
                for u in range(3):
                    step(0, u, first=(u == 0))
                with eng.Fori(0, NE // 4 - 1) as i:
                    for u in range(3, 7):
                        step(i, u)
                step(NE // 4 - 1, 3, last=True)
                evac_hT(NE - 1, 1)
                evac_y(NE - 1, 1, 16 * ((NE - 1) // 2))
                n_ovf = eng.value_load(ovf_id[0:1, OVF:OVF + 1], min_val=0, max_val=OVF)
                with eng.If(n_ovf > 0):
                    eng.wait_ge(S(f"y_stored{l}0"), 16 * NE // 2)
                    with eng.Fori(0, OVF) as j:
                        eng.wait_ge(S(f"ov_turn{l}"), OV_STEPS * (j + 1) + 1)
                        eng.tensor_copy(xeT[:, 0, 4:8, :], bank[1][:, :].rearrange("p (c n) -> p c n", c=4)).then_inc(S(f"ov_turn{l}"), 1)
                        eng.wait_ge(S(f"ov_turn{l}"), OV_STEPS * (j + 1) + 5)
                        eng.tensor_tensor(hsb[:, 0, :], ssb[:, 0, :], bank[2][:, F:2 * F], ALU.mult).then_inc(S(f"ov_turn{l}"), 1)
                        eng.wait_ge(S(f"ov_turn{l}"), OV_STEPS * (j + 1) + 7)
                        eng.tensor_copy(hT[:, 0, :, :], bank[4][:, 0:F].rearrange("p (c n) -> p c n", c=FC)).then_inc(S(f"ov_turn{l}"), 1)
                        eng.wait_ge(S(f"ov_turn{l}"), OV_STEPS * (j + 1) + 9)
                        eng.tensor_copy(ysb[:, 0, BLK:D], bank[6][:, :]).then_inc(S(f"ov_turn{l}"), 1)
                for t in range(NT):
                    eng.wait_ge(S(f"gated{l}"), t + 1)
                    y1, y2 = gy[:, t % 2, 0, :], gy[:, t % 2, 1, :]
                    link(eng.scalar_tensor_tensor(y1, y2, gates[:, t, 1:2], y1, ALU.mult, ALU.add))
                    eng.scalar_tensor_tensor(xres[:, t, :], xres[:, t, :], ALPHA, y1, ALU.mult, ALU.add).then_inc(S(f"mixed{l}"), 1)
                    eng.wait_ge(S(f"mixed{l}"), t + 1)
                    norm(l, 1, t)
                    if l + 1 < DEPTH and t >= 1:
                        evac_x_tile(f"{l}1", t - 1)
                if l + 1 < DEPTH:
                    evac_x_tile(f"{l}1", NT - 1)


_INS = ["x", "ln_gain", "ln_bias", "swa_w_in", "swa_sinks", "swa_w_o", "fox_w_in", "fox_b_f", "fox_w_o",
        "w_router", "b_router", "w_gate", "w_up", "w_down"]


def kernel(**inputs):
    import numpy as np
    import concourse.bacc as bacc
    from concourse.bass_utils import run_bass_kernel_spmd

    half = ROT // 2
    inv_freq = np.power(np.float32(500000.0), -np.arange(half, dtype=np.float32) * np.float32(2.0 / ROT)).astype(np.float32)
    ang = np.arange(SEQ, dtype=np.float32)[:, None] * inv_freq[None, :]
    rope = np.stack([np.tile(np.cos(ang), 2), np.tile(np.sin(ang), 2)], axis=1).astype(np.float32)

    nc = bacc.Bacc("TRN2", target_bir_lowering=False, num_devices=1)
    arrays, args = {}, []
    for name in _INS:
        a = np.ascontiguousarray(inputs[name])
        arrays[f"in_{name}"] = a
        args.append(nc.dram_tensor(f"in_{name}", a.shape, mybir.dt.from_np(a.dtype), kind="ExternalInput").ap())
    arrays["rope"] = rope
    args.append(nc.dram_tensor("rope", rope.shape, mybir.dt.float32, kind="ExternalInput").ap())
    args.append(nc.dram_tensor("out", (1, SEQ, D), mybir.dt.float32, kind="ExternalOutput").ap())
    trunk(nc, *args)
    r = run_bass_kernel_spmd(nc, [arrays], core_ids=[0])
    return r.results[0]["out"]
```

```python
import concourse.bass as bass
from concourse import mybir
from contextlib import ExitStack

P = 128
SEQ, D = 512, 1024
HD = 64
NH = D // HD
NKV = NH // 4
WINDOW = 128
NT = SEQ // P
KC = D // P
BLK = 512
NE, NG, TOPK = 16, 4, 2
EPG = NE // NG
F = D // 4
FC = F // P
ROT = HD // 4
DEPTH = 2
ALPHA = (2.0 * DEPTH) ** 0.25
LN_EPS = 1e-5
SCALE = HD ** -0.5
NEG = -1e30
CAP = P
OVF = SEQ * TOPK // (CAP + 1)
SLOTS = (NE + OVF) * CAP
PAIRS = NH // 2
UNITS = NH * NT
RING = 4
SLOT_WORDS = KC * BLK + FC * D
IN_BLOCKS = (3, 6)
OUT_BLOCKS = 2
IN_USE = (0, IN_BLOCKS[0] + OUT_BLOCKS + NE)
OUT_USE = tuple(IN_USE[l] + IN_BLOCKS[l] for l in range(DEPTH))
IN_ORDER = ((0, 1, 2), (4, 5, 0, 1, 2, 3))
EXP_USE = tuple(OUT_USE[l] + OUT_BLOCKS for l in range(DEPTH))


def trunk(nc, x, ln_gain, ln_bias, swa_w_in, swa_sinks, swa_w_o, fox_w_in, fox_b_f, fox_w_o,
          w_router, b_router, w_gate, w_up, w_down, rope, out):
    fp32, bf16, i32, u32 = mybir.dt.float32, mybir.dt.bfloat16, mybir.dt.int32, mybir.dt.uint32
    ALU = mybir.AluOpType
    ACT = mybir.ActivationFunctionType
    X = mybir.AxisListType.X

    ctx = ExitStack()
    with ctx:
        def sb(name, shape, dt=fp32):
            return ctx.enter_context(nc.sbuf_tensor(name, shape, dt))

        xres = sb("xres", [P, NT, D])
        xT = sb("xT", [P, KC, SEQ])
        ring = sb("ring", [P, RING, SLOT_WORDS])
        lnp = sb("lnp", [P, 2, D])
        ident = sb("ident", [P, P])
        before = sb("before", [P, P])
        ones = sb("ones", [P, P])
        before_b = sb("before_b", [P, P], bf16)
        ones_b = sb("ones_b", [P, P], bf16)
        asn_b = sb("asn_b", [P, NT * NE], bf16)
        band = sb("band", [P, 2, P])
        causal_b = sb("causal_b", [P, SEQ], bf16)
        ident_b = sb("ident_b", [P, P], bf16)
        cs = sb("cs", [P, NT, 2, ROT])
        sink = sb("sink", [P, NH])
        wr = sb("wr", [P, KC, NE])
        wf = sb("wf", [P, KC, NH])
        br = sb("br", [P, NE])
        bf = sb("bf", [NH, 1])
        stats = sb("stats", [P, NT, 2, 6])
        mv = sb("mv", [P, NT, 2])
        veps = sb("veps", [P, NT])
        rstd = sb("rstd", [P, NT])
        mhalf = sb("mhalf", [P, NT])
        nmax = sb("nmax", [P, 8])
        rsum = sb("rsum", [P, 8])
        rinv = sb("rinv", [P, 8])
        gates = sb("gates", [P, NT, 2])
        pos = sb("pos", [P, NT, 2], u32)
        ovf_id = sb("ovf_id", [1, 8], i32)
        arena = sb("arena", [P, 15700])

        def area(at, n, pattern=None, **kw):
            a = arena[:, at:at + n]
            return a.rearrange(pattern, **kw) if pattern else a

        QT = area(0, PAIRS * SEQ, "p (h t) -> p h t", h=PAIRS)
        KT = area(4096, PAIRS * SEQ, "p (h t) -> p h t", h=PAIRS)
        V = area(8192, NT * D, "p (t n) -> p t n", t=NT)
        sp = area(12288, 4 * 516, "p (b n) -> p b n", b=4)
        pT = area(14352, 2 * SEQ, "p (b n) -> p b n", b=2)
        rtmp = area(15376, 2 * 8 * ROT, "p (a n) -> p a n", a=2)
        tok = area(6144, 2 * BLK, "p (b n) -> p b n", b=2)
        zeros = area(10240, D)
        xTf = xT[:, :, :].rearrange("p c t -> p (c t)")
        cb = xTf[:, 0:2048].rearrange("p (b h n) -> p b h n", b=2, h=2)
        fz = area(12288, 4 * SEQ, "p (k n) -> p k n", k=4)
        def small(at, *shape):
            n = 1
            for s in shape:
                n *= s
            a = area(at, n)
            if len(shape) == 2:
                return a.rearrange("p (a b) -> p a b", a=shape[0])
            if len(shape) == 3:
                return a.rearrange("p (a b c) -> p a b c", a=shape[0], b=shape[1])
            return a
        lg, pr, tmp, msk, oh1, oh2, tot, slot = (small(14000 + 64 * k, NT, NE) for k in range(8))
        prg = area(14064, 64).rearrange("p (t g e) -> p t g e", t=NT, g=NG)
        pair = small(14512, NT, NG, 6)
        gs, gk = small(14608, NT, NG), small(14624, NT, NG)
        red = small(14640, 12, NT)
        ext, inc, dlt = (small(14700 + 16 * k, NE) for k in range(3))
        posf = small(14800, NT, 2)
        cmp7 = small(14840, OVF, NE)
        w4 = sb("w4", [P, NG])
        w16 = sb("w16", [P, NE])
        e128 = sb("e128", [P, NE])
        j7 = sb("j7", [P, OVF])
        xe = area(0, 4 * D, "p (b n) -> p b n", b=4)
        xeT = area(4096, 2 * KC * P, "p (b c n) -> p b c n", b=2, c=KC)
        ssb = area(6144, 2 * F, "p (b n) -> p b n", b=2)
        hsb = area(6656, 2 * F, "p (b n) -> p b n", b=2)
        hT = area(7168, 2 * FC * P, "p (b c n) -> p b c n", b=2, c=FC)
        ysb = area(7680, 2 * D, "p (b n) -> p b n", b=2)
        gy = area(9728, 4 * D, "p (b k n) -> p b k n", b=2, k=2)

        bank = [ctx.enter_context(nc.psum_tensor(f"bank{i}", [P, 512], fp32)) for i in range(8)]

        xs = nc.dram_tensor("xs", [SLOTS, D], fp32).ap()
        ys = nc.dram_tensor("ys", [SLOTS, D], fp32).ap()
        cd = nc.dram_tensor("cd", [NH, SEQ], fp32).ap()
        xs_t = xs.rearrange("(e p) d -> e p d", p=CAP)
        ys_t = ys.rearrange("(e p) d -> e p d", p=CAP)

        sems = {}

        def S(name):
            if name not in sems:
                sems[name] = ctx.enter_context(nc.semaphore(name))
            return sems[name]

        def chain(eng, name):
            n = [0]

            def link(ins):
                n[0] += 1
                ins.then_inc(S(name), 1)
                eng.wait_ge(S(name), n[0])
            return link

        def slot_in(k):
            return ring[:, k % RING, 0:KC * BLK].rearrange("p (c n) -> p c n", c=KC)

        def slot_down(k):
            return ring[:, k % RING, KC * BLK:SLOT_WORDS].rearrange("p (c n) -> p c n", c=FC)

        def weights_here(eng, k, more=0):
            eng.wait_ge(S(f"w_loaded{k % RING}"), ring_count(k) + more)

        def n_dmas(k):
            return 3 if any(EXP_USE[l] <= k < EXP_USE[l] + NE for l in range(DEPTH)) else 1

        def ring_count(k):
            return 16 * sum(n_dmas(j) for j in range(k % RING, k + 1, RING))

        OV_STEPS = 11
        UNIT = [(hp, n, half) for hp in range(PAIRS) for n in range(NT) for half in range(2)]
        GROUPS = (IN_BLOCKS[0] * NT, 4 * 4 + 2 * NT)

        def s_bank(u):
            return bank[(0, 1, 2, 7)[u % 4]]

        block = ctx.enter_context(nc.Block())

        @block.sync
        def _(eng):
            for t in range(NT):
                eng.dma_start(xres[:, t, :], x[0, t * P:(t + 1) * P, :]).then_inc(S(f"x_in{t}"), 16)

            def wait_used(k):
                l = 0 if k < IN_USE[1] else 1
                if k < OUT_USE[l]:
                    j = k - IN_USE[l]
                    eng.wait_ge(S(f"proj_done{l}"), 4 * (j + 1) if l == 0 else max(2 * NT, 4 * (j + 1)))
                elif k < EXP_USE[l]:
                    eng.wait_ge(S(f"wo_done{l}"), OUT_BLOCKS * (NT - 1) + k - OUT_USE[l] + 1)
                else:
                    eng.wait_ge(S(f"y_done{l}"), k - EXP_USE[l] + 1)

            def load_block(k, src):
                if k >= RING:
                    wait_used(k - RING)
                eng.dma_start(slot_in(k), src.rearrange("(c p) n -> p c n", p=P)).then_inc(S(f"w_loaded{k % RING}"), 16)

            def load_expert(s, w, e, sem):
                gu = slot_in(s)
                eng.dma_start(gu[:, :, 0:F], w_gate[w, e].rearrange("(c p) f -> p c f", p=P)).then_inc(sem, 16)
                eng.dma_start(gu[:, :, F:2 * F], w_up[w, e].rearrange("(c p) f -> p c f", p=P)).then_inc(sem, 16)
                eng.dma_start(slot_down(s), w_down[w, e].rearrange("(c p) n -> p c n", p=P)).then_inc(sem, 16)

            for l, (w_in, w_o) in enumerate(((swa_w_in[0], swa_w_o[0]), (fox_w_in[0], fox_w_o[0]))):
                for j in range(IN_BLOCKS[l]):
                    c = IN_ORDER[l][j]
                    load_block(IN_USE[l] + j, w_in[:, BLK * c:BLK * (c + 1)])
                    if l == 0 and j == 0:
                        eng.dma_start(cs[:, :, :, :], rope.rearrange("(t p) a n -> p t a n", p=P)).then_inc(S("const_in"), 16)
                        eng.dma_start(sink[:, :], swa_sinks[0].partition_broadcast(P)).then_inc(S("const_in"), 16)
                        eng.dma_start(wr[:, :, :], w_router.rearrange("(c p) n -> p c n", p=P)).then_inc(S("const_in"), 16)
                        eng.dma_start(br[:, :], b_router.partition_broadcast(P)).then_inc(S("const_in"), 16)
                        eng.dma_start(bf[:, :], fox_b_f.rearrange("a h -> h a")).then_inc(S("const_in"), 16)
                        eng.dma_start(wf[:, :, :], fox_w_in[0][:, 3 * D:3 * D + NH].rearrange("(c p) n -> p c n", p=P)).then_inc(S("const_in"), 16)
                for j in range(OUT_BLOCKS):
                    load_block(OUT_USE[l] + j, w_o[:, BLK * j:BLK * (j + 1)])
                for u in range(RING):
                    k = EXP_USE[l] + u
                    wait_used(k - RING)
                    load_expert(k, l, u, S(f"w_loaded{k % RING}"))
                with eng.Fori(1, NE // RING) as i:
                    for u in range(RING):
                        k = EXP_USE[l] + u
                        eng.wait_ge(S(f"y_done{l}"), RING * i + u - (RING - 1))
                        load_expert(k, l, RING * i + u, S(f"w_loaded{k % RING}"))
                eng.wait_ge(S(f"routed{l}"), 1)
                n_ovf = eng.value_load(ovf_id[0:1, OVF:OVF + 1], min_val=0, max_val=OVF)
                k = EXP_USE[l] + NE
                with eng.If(n_ovf > 0):
                    wait_used(k - RING)
                    with eng.Fori(0, OVF) as j:
                        e = eng.value_load(ovf_id[0:1, bass.ds(j, 1)], min_val=0, max_val=NE - 1)
                        eng.wait_ge(S(f"ov_turn{l}"), OV_STEPS * (j + 1))
                        load_expert(k, l, e, S(f"ov_in{l}"))
                        eng.dma_start(xe[:, 0, :], xs_t[j + NE]).then_inc(S(f"ov_in{l}"), 16)
                        eng.wait_ge(S(f"ov_turn{l}"), OV_STEPS * (j + 1) + 11)
                        eng.dma_start(ys_t[j + NE], ysb[:, 0, :]).then_inc(S(f"ov_stored{l}"), 16)
            for t in range(NT):
                eng.wait_ge(S(f"x_ready{l}1"), t + 1)
                eng.dma_start(out[0, t * P:(t + 1) * P, :], xres[:, t, :]).then_inc(S("out_done"), 16)
            eng.wait_ge(S("out_done"), 16 * NT)

        @block.gpsimd
        def _(eng):
            link = chain(eng, "pool_step")
            link(eng.memset(ident[:, :], 0.0))
            link(eng.affine_select(out=ident[:, :], in_=ident[:, :], compare_op=ALU.not_equal, fill=1.0,
                                   base=0, pattern=[[-1, P]], channel_multiplier=1))
            link(eng.memset(ones[:, :], 1.0))
            link(eng.affine_select(out=before[:, :], in_=ones[:, :], compare_op=ALU.is_ge, fill=0.0,
                                   base=-1, pattern=[[1, P]], channel_multiplier=-1))
            link(eng.memset(band[:, :, :], 0.0))
            link(eng.memset(causal_b[:, :], 0.0))
            link(eng.affine_select(out=band[:, 0, :], in_=band[:, 0, :], compare_op=ALU.is_ge, fill=NEG / SCALE,
                                   base=-1, pattern=[[1, P]], channel_multiplier=-1))
            link(eng.affine_select(out=band[:, 1, :], in_=band[:, 1, :], compare_op=ALU.is_ge, fill=NEG / SCALE,
                                   base=0, pattern=[[-1, P]], channel_multiplier=1))
            link(eng.iota(w4[:, :], [[-1, NG]], base=NG, channel_multiplier=0, allow_small_or_imprecise_dtypes=True))
            link(eng.iota(w16[:, :], [[-1, NE]], base=NE, channel_multiplier=0, allow_small_or_imprecise_dtypes=True))
            link(eng.iota(e128[:, :], [[CAP, NE]], base=0, channel_multiplier=0, allow_small_or_imprecise_dtypes=True))
            link(eng.iota(j7[:, :], [[1, OVF]], base=0, channel_multiplier=0, allow_small_or_imprecise_dtypes=True))
            link(eng.memset(mhalf[:, :], -0.5))
            link(eng.tensor_copy(before_b[:, :], before[:, :]))
            link(eng.tensor_copy(ones_b[:, :], ones[:, :]))
            link(eng.tensor_copy(ident_b[:, :], ident[:, :]))
            link(eng.tensor_copy(causal_b[:, SEQ - P:SEQ], band[:, 1, :]))
            eng.memset(zeros, 0.0).then_inc(S("consts"), 1)
            eng.wait_ge(S("consts"), 1)
            eng.wait_ge(S(f"w_loaded{2}"), 16)
            eng.dma_start(xs.rearrange("(e p) d -> p e d", p=CAP),
                          zeros.unsqueeze(1).to_broadcast([P, NE + OVF, D])).then_inc(S("cleared"), 16)
            eng.dma_start(ys.rearrange("(e p) d -> p e d", p=CAP)[:, NE:NE + OVF, :],
                          zeros.unsqueeze(1).to_broadcast([P, OVF, D])).then_inc(S("cleared"), 16)
            eng.wait_ge(S("cleared"), 32)
            eng.drain().then_inc(S("zeros_free"), 1)

            def load_norm(l, w):
                eng.dma_start(lnp[:, 0, :], ln_gain[l, w].partition_broadcast(P)).then_inc(S("ln_in"), 16)
                eng.dma_start(lnp[:, 1, :], ln_bias[l, w].partition_broadcast(P)).then_inc(S("ln_in"), 16)

            def norm_rstd(l, w, gather=None):
                for t in range(NT):
                    eng.wait_ge(S(f"ln_stats{l}{w}"), t + 1)
                    link(eng.tensor_scalar(veps[:, t:t + 1], mv[:, t, 1:2], LN_EPS, None, ALU.add))
                    eng.tensor_tensor(rstd[:, t:t + 1], veps[:, t:t + 1], mhalf[:, t:t + 1], ALU.pow).then_inc(S(f"rstd{l}{w}"), 1)
                    if gather and t + 2 < NT:
                        gather(t + 2)
                if (l, w) != (DEPTH - 1, 1):
                    eng.wait_ge(S(f"x_ready{l}{w}"), NT)
                    load_norm(*((l, 1) if w == 0 else (l + 1, 0)))

            load_norm(0, 0)
            for l in range(DEPTH):
                if l == 1:
                    eng.wait_ge(S("decay"), 1)
                    eng.dma_start(cd, fz[0:NH, 3, :]).then_inc(S("cd_out"), 16)
                    eng.wait_ge(S("cd_out"), 16)
                    eng.wait_ge(S(f"proj_done{l}"), GROUPS[l])
                    for hp in range(PAIRS):
                        if hp >= 2:
                            eng.wait_ge(S(f"sp_ready{l}"), 2 * NT * (hp - 1))
                        eng.dma_start(cb[:, hp % 2, :, :], cd[2 * hp:2 * hp + 2].partition_broadcast(P)).then_inc(S(f"cb_in{hp % 2}"), 16)
                norm_rstd(l, 0)
                eng.wait_ge(S(f"routed{l}"), 1)
                for t in range(NT):
                    for k in range(TOPK):
                        eng.indirect_dma_start(xs, bass.IndirectOffsetOnAxis(ap=pos[:, t, k:k + 1], axis=0),
                                               xres[:, t, :], None).then_inc(S(f"scattered{l}"), 16)
                for b in range(2):
                    eng.wait_ge(S(f"y_stored{l}{b}"), 16 * NE // 2)
                n_ovf = eng.value_load(ovf_id[0:1, OVF:OVF + 1], min_val=0, max_val=OVF)
                with eng.If(n_ovf > 0):
                    eng.sem_inc(S(f"ov_turn{l}"), OV_STEPS)
                    with eng.Fori(0, OVF) as j:
                        eng.wait_ge(S(f"ov_stored{l}"), 16 * j + 16)
                def gather(t):
                    if t >= 2:
                        eng.wait_ge(S(f"mixed{l}"), t - 1)
                    for k in range(TOPK):
                        eng.indirect_dma_start(gy[:, t % 2, k, :], None, ys,
                                               bass.IndirectOffsetOnAxis(ap=pos[:, t, k:k + 1], axis=0)).then_inc(S(f"gy_in{l}{t % 2}"), 16)
                gather(0)
                gather(1)
                norm_rstd(l, 1, gather)

        @block.tensor
        def _(eng):
            def turn_x(t, a):
                if a == "in":
                    eng.wait_ge(S(f"x_in{t}"), 16)
                else:
                    eng.wait_ge(S(f"x_ready{a}"), t + 1)
                if t >= 1:
                    eng.wait_ge(S(f"xt_act{a}"), t)
                    eng.wait_ge(S(f"xt_dve{a}"), t)
                for c in range(KC):
                    mm = eng.transpose(bank[3 + c // 4][:, (c % 4) * P:(c % 4 + 1) * P],
                                       xres[:, t, c * P:(c + 1) * P], ident[:, :])
                mm.then_inc(S(f"xt_done{a}"), 1)

            eng.wait_ge(S("consts"), 1)
            for t in range(NT):
                turn_x(t, "in")
            for l in range(DEPTH):
                def xT_here(a, t):
                    eng.wait_ge(S(f"xt_act{a}"), t + 1)
                    eng.wait_ge(S(f"xt_dve{a}"), t + 1)

                def project(k, lhs, rhs, use):
                    if k >= 2:
                        eng.wait_ge(S(f"proj_free{l}{k % 2}"), k // 2)
                    weights_here(eng, use)
                    for c in range(KC):
                        mm = eng.matmul(bank[k % 2][:, :], lhs(c), rhs(c), start=(c == 0), stop=(c == KC - 1))
                    mm.then_inc(S(f"proj_done{l}"), 1)

                if l == 0:
                    def turn_heads(k):
                        eng.wait_ge(S("roped"), k + 1)
                        if k >= 2:
                            eng.wait_ge(S("qkT_free"), k - 1)
                        for i in range(4):
                            mm = eng.transpose(bank[5 + k % 2][:, i * P:(i + 1) * P], tok[:, k % 2, i * P:(i + 1) * P], ident[:, :])
                        mm.then_inc(S("qkT_done"), 1)

                    for j in range(IN_BLOCKS[0]):
                        for t in range(NT):
                            k = NT * j + t
                            w = slot_in(j)
                            xT_here("in", t)
                            project(k, lambda c: xT[:, c, t * P:(t + 1) * P], lambda c: w[:, c, :], j)
                            if k >= 1:
                                turn_heads(k - 1)
                    turn_heads(GROUPS[0] - 1)
                    eng.wait_ge(S("qkT_free"), GROUPS[0])
                else:
                    for t in range(NT):
                        turn_x(t, "01")
                        xT_here("01", t)
                        for b in range(2):
                            w = slot_in(IN_USE[1] + b)
                            project(2 * t + b, lambda c: xT[:, c, t * P:(t + 1) * P], lambda c: w[:, c, :], IN_USE[1] + b)
                    eng.wait_ge(S("const_in"), 96)
                    for c in range(KC):
                        mm = eng.matmul(bank[7][0:NH, :], wf[:, c, :], xT[:, c, :], start=(c == 0), stop=(c == KC - 1))
                    mm.then_inc(S("forget"), 1)
                    for j in range(2, IN_BLOCKS[1]):
                        w = slot_in(IN_USE[1] + j)
                        for i in range(4):
                            project(4 * j + i, lambda c: w[:, c, i * P:(i + 1) * P], lambda c: xT[:, c, :], IN_USE[1] + j)
                    for b in range(2):
                        eng.wait_ge(S(f"proj_free{l}{b}"), GROUPS[1] // 2)

                def keys(n):
                    return (max(n - 1, 0), n + 1) if l == 0 else (0, n + 1)

                def scores(u):
                    hp, n, half = UNIT[u]
                    k0, k1 = keys(n)
                    if u >= 4:
                        eng.wait_ge(S(f"sp_ready{l}"), u - 3)
                    r = slice(HD * half, HD * half + HD)
                    kp = (2 * hp + half) // (NH // NKV) if l == 0 else hp
                    nk = (k1 - k0) * P
                    if l == 1:
                        eng.matmul(s_bank(u)[:, 0:nk], ident_b[:, :], causal_b[:, SEQ - nk:SEQ], start=True, stop=False)
                    eng.matmul(s_bank(u)[:, 0:nk], QT[r, hp, n * P:(n + 1) * P], KT[r, kp, k0 * P:k1 * P],
                               start=(l == 0), stop=True).then_inc(S(f"s_done{l}"), 1)

                def turn_probs(u):
                    hp, n, half = UNIT[u]
                    k0, k1 = keys(n)
                    eng.wait_ge(S(f"p_ready{l}"), u + 1)
                    if u >= 2:
                        eng.wait_ge(S(f"pT_ready{l}{half}"), u // 2)
                    for i in range(k1 - k0):
                        mm = eng.transpose(bank[3 + u % 2][:, i * P:(i + 1) * P], sp[:, u % 4, i * P:(i + 1) * P], ident[:, :])
                    mm.then_inc(S(f"pT_done{l}"), 1)

                def mix(u):
                    hp, n, half = UNIT[u]
                    k0, k1 = keys(n)
                    k = u // 2
                    eng.wait_ge(S(f"pT_ready{l}{half}"), k + 1)
                    if k >= 2 and half == 0:
                        eng.wait_ge(S(f"aT_ready{l}"), k - 1)
                    v = HD * ((2 * hp + half) // (NH // NKV) if l == 0 else 2 * hp + half)
                    for i in range(k1 - k0):
                        mm = eng.matmul(bank[5 + k % 2][HD * half:HD * half + HD, 0:P], V[:, k0 + i, v:v + HD],
                                        pT[:, u % 2, i * P:(i + 1) * P], start=(i == 0), stop=(i == k1 - k0 - 1))
                    mm.then_inc(S(f"pv_done{l}"), 1)

                for u in range(3):
                    scores(u)
                for u in range(UNITS):
                    if u + 3 < UNITS:
                        scores(u + 3)
                    turn_probs(u)
                    if u >= 1:
                        mix(u - 1)
                mix(UNITS - 1)

                def route(t):
                    xT_here(f"{l}0", t)
                    if t == 0:
                        eng.wait_ge(S("const_in"), 96)
                    for c in range(KC):
                        mm = eng.matmul(bank[7][:, t * NE:(t + 1) * NE], xT[:, c, t * P:(t + 1) * P], wr[:, c, :],
                                        start=(c == 0), stop=(c == KC - 1))
                    mm.then_inc(S(f"logits{l}"), 1)

                eng.wait_ge(S(f"aT_ready{l}"), UNITS // 2)
                for t in range(NT):
                    for b in range(OUT_BLOCKS):
                        g = OUT_BLOCKS * t + b
                        if g >= 2:
                            eng.wait_ge(S(f"res_done{l}"), g - 1)
                        weights_here(eng, OUT_USE[l] + b)
                        w = slot_in(OUT_USE[l] + b)
                        for c in range(KC):
                            mm = eng.matmul(bank[b][:, :], QT[:, c, t * P:(t + 1) * P], w[:, c, :], start=(c == 0), stop=(c == KC - 1))
                        mm.then_inc(S(f"wo_done{l}"), 1)
                        if t >= 1 and b == 0:
                            turn_x(t - 1, f"{l}0")
                    if t >= 1:
                        route(t - 1)
                turn_x(NT - 1, f"{l}0")
                route(NT - 1)
                eng.wait_ge(S(f"assigned{l}"), 1)
                eng.matmul(bank[2][:, 0:NT * NE], before_b[:, :], asn_b[:, :], start=True, stop=True)
                eng.matmul(bank[6][:, 0:NT * NE], ones_b[:, :], asn_b[:, :], start=True, stop=True).then_inc(S(f"ranked{l}"), 1)

                def turn_rows(b):
                    for c in range(KC):
                        mm = eng.transpose(bank[c // 4][:, (c % 4) * P:(c % 4 + 1) * P], xe[:, b, c * P:(c + 1) * P], ident[:, :])
                    return mm

                def gate_up(b, use):
                    w = slot_in(use)
                    for c in range(KC):
                        mm = eng.matmul(bank[2 + b][:, :], xeT[:, b, c, :], w[:, c, :], start=(c == 0), stop=(c == KC - 1))
                    return mm

                def turn_h(b):
                    for c in range(FC):
                        mm = eng.transpose(bank[4][:, c * P:(c + 1) * P], hsb[:, b, c * P:(c + 1) * P], ident[:, :])
                    return mm

                def down(b, use):
                    w = slot_down(use)
                    for half in range(2):
                        for c in range(FC):
                            mm = eng.matmul(bank[5 + half][:, :], hT[:, b, c, :], w[:, c, half * BLK:(half + 1) * BLK],
                                            start=(c == 0), stop=(c == FC - 1))
                    return mm

                def step(i, u, first=False, last=False):
                    use = EXP_USE[l] + u
                    e = 4 * i + u
                    eng.wait_ge(S(f"xeT_act{l}"), e + 1)
                    eng.wait_ge(S(f"xeT_dve{l}"), e + 1)
                    eng.wait_ge(S(f"w_loaded{use % RING}"), 48 * i + ring_count(use))
                    gate_up(u % 2, use).then_inc(S(f"gu_done{l}"), 1)
                    if not first:
                        eng.wait_ge(S(f"h_ready{l}"), e)
                        turn_h((u - 1) % 2).then_inc(S(f"hT_done{l}"), 1)
                    if not last:
                        eng.wait_ge(S(f"xe_in{l}{(u + 1) % 4}"), 16 * i + 16 * ((u + 1) // 4) + 16)
                        turn_rows((u + 1) % 4).then_inc(S(f"xeT_done{l}"), 1)
                    if not first:
                        down_of(e - 1, (u - 1) % 2, use - 1, u > 1 or not isinstance(i, int) or i > 0)

                def down_of(e, b, use, reused):
                    eng.wait_ge(S(f"hT_ready{l}"), e + 1)
                    if reused:
                        eng.wait_ge(S(f"y_act{l}"), e)
                        eng.wait_ge(S(f"y_dve{l}"), e)
                    down(b, use).then_inc(S(f"y_done{l}"), 1)

                eng.wait_ge(S(f"xe_in{l}0"), 16)
                turn_rows(0).then_inc(S(f"xeT_done{l}"), 1)
                step(0, 0, first=True)
                step(0, 1)
                with eng.Fori(0, NE // 4 - 1) as i:
                    for u in range(2, 6):
                        step(i, u)
                for u in range(2, 4):
                    step(NE // 4 - 1, u, last=(u == 3))
                eng.wait_ge(S(f"h_ready{l}"), NE)
                turn_h(1).then_inc(S(f"hT_done{l}"), 1)
                down_of(NE - 1, 1, EXP_USE[l] + NE - 1, True)
                n_ovf = eng.value_load(ovf_id[0:1, OVF:OVF + 1], min_val=0, max_val=OVF)
                with eng.If(n_ovf > 0):
                    eng.wait_ge(S(f"y_act{l}"), NE)
                    eng.wait_ge(S(f"y_dve{l}"), NE)
                    with eng.Fori(0, OVF) as j:
                        eng.wait_ge(S(f"ov_in{l}"), 64 * j + 64)
                        turn_rows(0).then_inc(S(f"ov_turn{l}"), 1)
                        eng.wait_ge(S(f"ov_turn{l}"), OV_STEPS * (j + 1) + 3)
                        gate_up(0, EXP_USE[l] + NE).then_inc(S(f"ov_turn{l}"), 1)
                        eng.wait_ge(S(f"ov_turn{l}"), OV_STEPS * (j + 1) + 6)
                        turn_h(0).then_inc(S(f"ov_turn{l}"), 1)
                        eng.wait_ge(S(f"ov_turn{l}"), OV_STEPS * (j + 1) + 8)
                        down(0, EXP_USE[l] + NE).then_inc(S(f"ov_turn{l}"), 1)

        @block.scalar
        def _(eng):
            def evac_x(a, t):
                eng.wait_ge(S(f"xt_done{a}"), t + 1)
                eng.copy(xT[:, 0:4, t * P:(t + 1) * P], bank[3][:, :].rearrange("p (c n) -> p c n", c=4)).then_inc(S(f"xt_act{a}"), 1)

            for t in range(NT):
                evac_x("in", t)
            for l in range(DEPTH):
                if l == 0:
                    for k in range(GROUPS[0]):
                        eng.wait_ge(S("proj_done0"), k + 1)
                        if k >= 2:
                            eng.wait_ge(S("qkT_done"), k - 1)
                        j, t = k // NT, k % NT
                        b = bank[k % 2]
                        if j < 2:
                            cp = eng.copy(tok[:, k % 2, :], b[:, :])
                        else:
                            if t == 2:
                                eng.wait_ge(S("zeros_free"), 1)
                            eng.copy(V[:, t, 0:F], b[:, F:2 * F])
                            cp = eng.copy(tok[:, k % 2, :].rearrange("p (h a d) -> p h a d", a=2, d=HD)[:, :, 0, :],
                                          b[:, 0:F].rearrange("p (h d) -> p h d", d=HD))
                        cp.then_inc(S(f"proj_free0{k % 2}"), 1)
                else:
                    eng.wait_ge(S("fz_abs"), 1)
                    eng.activation(fz[0:NH, 1, :], fz[0:NH, 1, :], ACT.Exp, scale=-1.0).then_inc(S("act_step"), 1)
                    eng.wait_ge(S("act_step"), 1)
                    eng.activation(fz[0:NH, 1, :], fz[0:NH, 1, :], ACT.Ln, bias=1.0).then_inc(S("fz_ln"), 1)
                    for k in range(2 * NT, GROUPS[1], 2):
                        eng.wait_ge(S("proj_done1"), k + 1)
                        j, i = k // 4 - 2, k % 4
                        dst = QT[:, 4 * j + i, :] if j < 2 else KT[:, 4 * (j - 2) + i, :]
                        eng.copy(dst, bank[0][:, :]).then_inc(S("proj_free10"), 1)

                def expo(u):
                    hp, n, half = UNIT[u]
                    nk = P * (min(n, 1) + 1) + 1 if l == 0 else P * (n + 1)
                    eng.wait_ge(S(f"sp_ready{l}"), u + 1)
                    eng.activation(sp[:, u % 4, 0:nk], sp[:, u % 4, 0:nk], ACT.Exp, bias=nmax[:, u % 8:u % 8 + 1], scale=-1.0,
                                   accum_out=rsum[:, u % 8:u % 8 + 1]).then_inc(S(f"exp_done{l}"), 1)

                expo(0)
                expo(1)
                for u in range(UNITS):
                    if u + 2 < UNITS:
                        expo(u + 2)
                    hp, n, half = UNIT[u]
                    if half == 0:
                        nk = P * (min(n, 1) + 1) if l == 0 else P * (n + 1)
                        eng.wait_ge(S(f"pT_done{l}"), u + 1)
                        if u >= 2:
                            eng.wait_ge(S(f"pv_done{l}"), u - 1)
                        eng.copy(pT[:, u % 2, 0:nk], bank[3 + u % 2][:, 0:nk]).then_inc(S(f"pT_ready{l}0"), 1)

                for t in range(NT):
                    evac_x(f"{l}0", t)
                eng.wait_ge(S(f"shifted{l}"), 1)
                eng.activation(pr, lg, ACT.Exp).then_inc(S(f"expd{l}"), 1)

                def load_rows(e, b):
                    eng.dma_start(xe[:, b, :], xs_t[e]).then_inc(S(f"xe_in{l}{b}"), 16)

                def store_rows(e, b):
                    eng.wait_ge(S(f"y_dve{l}"), e + 1)
                    eng.wait_ge(S(f"y_act{l}"), e + 1)
                    eng.dma_start(ys_t[e], ysb[:, b, :]).then_inc(S(f"y_stored{l}{b}"), 16)

                def evac_rows(e, b):
                    eng.wait_ge(S(f"xeT_done{l}"), e + 1)
                    eng.copy(xeT[:, b, 0:4, :], bank[0][:, :].rearrange("p (c n) -> p c n", c=4)).then_inc(S(f"xeT_act{l}"), 1)

                def silu(e, b):
                    eng.wait_ge(S(f"gu_done{l}"), e + 1)
                    eng.activation(ssb[:, b, :], bank[2 + b][:, 0:F], ACT.Silu).then_inc(S(f"silu{l}"), 1)

                def evac_y(e, b, stored):
                    eng.wait_ge(S(f"y_done{l}"), e + 1)
                    if stored is not None:
                        eng.wait_ge(S(f"y_stored{l}{b}"), stored)
                    eng.copy(ysb[:, b, 0:BLK], bank[5][:, :]).then_inc(S(f"y_act{l}"), 1)

                def step(i, u, first=False, last=False):
                    e = 4 * i + u
                    silu(e, u % 2)
                    if not last:
                        evac_rows(e + 1, (u + 1) % 2)
                        if not isinstance(i, int) or e + 5 < NE:
                            load_rows(e + 5, (u + 1) % 4)
                    if not first:
                        started = not isinstance(i, int) or 4 * i + u - 1 >= 2
                        evac_y(e - 1, (u - 1) % 2, 32 * i + 16 * ((u - 1) // 2) if started else None)
                        store_rows(e - 1, (u - 1) % 2)

                eng.wait_ge(S(f"scattered{l}"), 16 * NT * TOPK)
                for b in range(4):
                    load_rows(b, b)
                evac_rows(0, 0)
                load_rows(4, 0)
                for u in range(3):
                    step(0, u, first=(u == 0))
                with eng.Fori(0, NE // 4 - 2) as i:
                    for u in range(3, 7):
                        step(i, u)
                for u in range(3, 8):
                    step(NE // 4 - 2, u, last=(u == 7))
                evac_y(NE - 1, 1, 16 * ((NE - 1) // 2))
                store_rows(NE - 1, 1)
                n_ovf = eng.value_load(ovf_id[0:1, OVF:OVF + 1], min_val=0, max_val=OVF)
                with eng.If(n_ovf > 0):
                    eng.wait_ge(S(f"y_stored{l}0"), 16 * NE // 2)
                    with eng.Fori(0, OVF) as j:
                        eng.wait_ge(S(f"ov_turn{l}"), OV_STEPS * (j + 1) + 1)
                        eng.copy(xeT[:, 0, 0:4, :], bank[0][:, :].rearrange("p (c n) -> p c n", c=4)).then_inc(S(f"ov_turn{l}"), 1)
                        eng.wait_ge(S(f"ov_turn{l}"), OV_STEPS * (j + 1) + 4)
                        eng.activation(ssb[:, 0, :], bank[2][:, 0:F], ACT.Silu).then_inc(S(f"ov_turn{l}"), 1)
                        eng.wait_ge(S(f"ov_turn{l}"), OV_STEPS * (j + 1) + 9)
                        eng.copy(ysb[:, 0, 0:BLK], bank[5][:, :]).then_inc(S(f"ov_turn{l}"), 1)
                def gate_first(t):
                    eng.wait_ge(S(f"gy_in{l}{t % 2}"), 32 * (t // 2 + 1))
                    eng.activation(gy[:, t % 2, 0, :], gy[:, t % 2, 0, :], ACT.Copy, scale=gates[:, t, 0:1]).then_inc(S(f"gated{l}"), 1)

                gate_first(0)
                gate_first(1)
                for t in range(NT):
                    if l + 1 < DEPTH:
                        evac_x(f"{l}1", t)
                    if t + 2 < NT:
                        gate_first(t + 2)
                    if l + 1 < DEPTH:
                        for b in range(2):
                            eng.wait_ge(S("proj_done1"), 2 * t + b + 1)
                            eng.copy(V[:, t, b * BLK:(b + 1) * BLK], bank[b][:, :]).then_inc(S(f"proj_free1{b}"), 1)

        @block.vector
        def _(eng):
            link = chain(eng, "dve_step")

            def evac_x_tile(a, t):
                eng.wait_ge(S(f"xt_done{a}"), t + 1)
                eng.tensor_copy(xT[:, 4:8, t * P:(t + 1) * P], bank[4][:, :].rearrange("p (c n) -> p c n", c=4)).then_inc(S(f"xt_dve{a}"), 1)

            norms = [0]

            def norm(l, w, t):
                v = xres[:, t, :]
                if t == 0:
                    norms[0] += 1
                    eng.wait_ge(S("ln_in"), 32 * norms[0])
                eng.bn_stats(stats[:, t, 0, :], xres[:, t, 0:BLK])
                link(eng.bn_stats(stats[:, t, 1, :], xres[:, t, BLK:D]))
                eng.bn_aggr(mv[:, t, :], stats[:, t, :, :].rearrange("p a b -> p (a b)")).then_inc(S(f"ln_stats{l}{w}"), 1)
                eng.wait_ge(S(f"ln_stats{l}{w}"), t + 1)
                link(eng.scalar_tensor_tensor(v, v, mv[:, t, 0:1], lnp[:, 0, :], ALU.subtract, ALU.mult))
                eng.wait_ge(S(f"rstd{l}{w}"), t + 1)
                eng.scalar_tensor_tensor(v, v, rstd[:, t:t + 1], lnp[:, 1, :], ALU.mult, ALU.add).then_inc(S(f"x_ready{l}{w}"), 1)

            for t in range(NT):
                evac_x_tile("in", t)
            eng.wait_ge(S("const_in"), 96)
            link(eng.tensor_scalar(sink[:, :], sink[:, :], -1.0, None, ALU.mult))
            for l in range(DEPTH):
                if l == 0:
                    def evac_heads(k):
                        eng.wait_ge(S("qkT_done"), k + 1)
                        j, t = k // NT, k % NT
                        dst = QT[:, 4 * j:4 * j + 4, :] if j < 2 else KT[:, 0:4, :]
                        eng.tensor_copy(dst[:, :, t * P:(t + 1) * P],
                                        bank[5 + k % 2][:, :].rearrange("p (h n) -> p h n", h=4)).then_inc(S("qkT_free"), 1)

                    for k in range(GROUPS[0]):
                        j, t = k // NT, k % NT
                        eng.wait_ge(S(f"proj_free0{k % 2}"), k // 2 + 1)
                        if j < 2:
                            nh, hv = 8, tok[:, k % 2, :].rearrange("p (h d) -> p h d", d=HD)
                        else:
                            kd = tok[:, k % 2, :].rearrange("p (h a d) -> p h a d", a=2, d=HD)
                            nh, hv = 4, kd[:, :, 0, :]
                        r = hv[:, :, 0:ROT]
                        if k >= 1:
                            eng.wait_ge(S("roped"), k)
                        tc = rtmp[:, 0, 0:nh * ROT].rearrange("p (h d) -> p h d", h=nh)
                        ts = rtmp[:, 1, 0:nh * ROT].rearrange("p (h d) -> p h d", h=nh)
                        eng.tensor_tensor(tc, r, cs[:, t, 0, :].unsqueeze(1).to_broadcast([P, nh, ROT]), ALU.mult)
                        link(eng.tensor_tensor(ts, r, cs[:, t, 1, :].unsqueeze(1).to_broadcast([P, nh, ROT]), ALU.mult))
                        h = ROT // 2
                        rot = eng.tensor_tensor(hv[:, :, 0:h], tc[:, :, 0:h], ts[:, :, h:ROT], ALU.subtract)
                        if j < 2:
                            eng.tensor_tensor(hv[:, :, h:ROT], tc[:, :, h:ROT], ts[:, :, 0:h], ALU.add).then_inc(S("roped"), 1)
                        else:
                            link(eng.tensor_tensor(hv[:, :, h:ROT], tc[:, :, h:ROT], ts[:, :, 0:h], ALU.add))
                            eng.tensor_copy(kd[:, :, 1, :], kd[:, :, 0, :]).then_inc(S("roped"), 1)
                        if k >= 1:
                            evac_heads(k - 1)
                    evac_heads(GROUPS[0] - 1)
                else:
                    eng.wait_ge(S("forget"), 1)
                    z, az, ls, c = (fz[0:NH, k, :] for k in range(4))
                    link(eng.tensor_scalar(z, bank[7][0:NH, :], bf[:, 0:1], None, ALU.add))
                    link(eng.tensor_scalar(az, z, -1.0, None, ALU.mult))
                    eng.tensor_tensor(az, az, z, ALU.max).then_inc(S("fz_abs"), 1)
                    link(eng.tensor_scalar(z, z, 0.0, None, ALU.min))
                    eng.wait_ge(S("fz_ln"), 1)
                    link(eng.tensor_tensor(ls, z, az, ALU.subtract))
                    link(eng.memset(z, 0.0))
                    link(eng.tensor_tensor_scan(c, ls, z, 0.0, ALU.add, ALU.add))
                    eng.tensor_scalar(c, c, -1.0 / SCALE, None, ALU.mult).then_inc(S("decay"), 1)
                    for k in range(2 * NT + 1, GROUPS[1], 2):
                        eng.wait_ge(S("proj_done1"), k + 1)
                        j, i = k // 4 - 2, k % 4
                        dst = QT[:, 4 * j + i, :] if j < 2 else KT[:, 4 * (j - 2) + i, :]
                        eng.tensor_copy(dst, bank[1][:, :]).then_inc(S("proj_free11"), 1)
                    eng.wait_ge(S("cd_out"), 16)

                def mask_and_max(u):
                    hp, n, half = UNIT[u]
                    h = 2 * hp + half
                    eng.wait_ge(S(f"s_done{l}"), u + 1)
                    if u >= 4:
                        eng.wait_ge(S(f"pT_done{l}"), u - 3)
                    s, o, m = s_bank(u), sp[:, u % 4, :], nmax[:, u % 8:u % 8 + 1]
                    if l == 0:
                        nk = P * (min(n, 1) + 1)
                        bias = band[:, :, :].rearrange("p a k -> p (a k)")[:, 2 * P - nk:2 * P]
                        eng.tensor_copy(o[:, nk:nk + 1], sink[:, h:h + 1])
                        eng.tensor_tensor_reduce(out=o[:, 0:nk], in0=s[:, 0:nk], in1=bias, scale=-SCALE,
                                                 scalar=sink[:, h:h + 1], op0=ALU.add, op1=ALU.min,
                                                 accum_out=m).then_inc(S("sp_ready0"), 1)
                    else:
                        if n == 0 and half == 0:
                            eng.wait_ge(S(f"cb_in{hp % 2}"), 16 * (hp // 2 + 1))
                        nk = P * (n + 1)
                        eng.tensor_tensor_reduce(out=o[:, 0:nk], in0=s[:, 0:nk], in1=cb[:, hp % 2, half, 0:nk],
                                                 scale=-SCALE, scalar=-NEG, op0=ALU.add, op1=ALU.min,
                                                 accum_out=m).then_inc(S("sp_ready1"), 1)

                def normalise(u):
                    hp, n, half = UNIT[u]
                    nk = P * (min(n, 1) + 1) if l == 0 else P * (n + 1)
                    eng.wait_ge(S(f"exp_done{l}"), u + 1)
                    link(eng.reciprocal(rinv[:, u % 8:u % 8 + 1], rsum[:, u % 8:u % 8 + 1]))
                    eng.tensor_scalar(sp[:, u % 4, 0:nk], sp[:, u % 4, 0:nk], rinv[:, u % 8:u % 8 + 1], None, ALU.mult).then_inc(S(f"p_ready{l}"), 1)

                def evac_out(k):
                    hp, n, _ = UNIT[2 * k]
                    eng.wait_ge(S(f"pv_done{l}"), 2 * k + 2)
                    eng.tensor_copy(QT[:, hp, n * P:(n + 1) * P], bank[5 + k % 2][:, 0:P]).then_inc(S(f"aT_ready{l}"), 1)

                mask_and_max(0)
                mask_and_max(1)
                normalise(0)
                for u in range(UNITS):
                    if u + 2 < UNITS:
                        mask_and_max(u + 2)
                    if u + 1 < UNITS:
                        normalise(u + 1)
                    hp, n, half = UNIT[u]
                    if half == 1:
                        nk = P * (min(n, 1) + 1) if l == 0 else P * (n + 1)
                        eng.wait_ge(S(f"pT_done{l}"), u + 1)
                        if u >= 2:
                            eng.wait_ge(S(f"pv_done{l}"), u - 1)
                        eng.tensor_copy(pT[:, u % 2, 0:nk], bank[3 + u % 2][:, 0:nk]).then_inc(S(f"pT_ready{l}1"), 1)
                    elif u >= 2:
                        evac_out(u // 2 - 1)
                evac_out(UNITS // 2 - 1)

                for t in range(NT):
                    for b in range(OUT_BLOCKS):
                        eng.wait_ge(S(f"wo_done{l}"), OUT_BLOCKS * t + b + 1)
                        v = xres[:, t, b * BLK:(b + 1) * BLK]
                        ins = eng.scalar_tensor_tensor(v, v, ALPHA, bank[b][:, :], ALU.mult, ALU.add)
                        ins.then_inc(S(f"res_done{l}"), 1)
                        if t >= 1 and b == 0:
                            evac_x_tile(f"{l}0", t - 1)
                    eng.wait_ge(S(f"res_done{l}"), OUT_BLOCKS * (t + 1))
                    norm(l, 0, t)
                evac_x_tile(f"{l}0", NT - 1)

                def over(a, n):
                    return a.unsqueeze(2).to_broadcast([P, a.shape[1], n])

                def tiles(a):
                    return a.unsqueeze(1).to_broadcast([P, NT, a.shape[1]])

                mx, sm, rs, gm, kb, v1, k1, v2, k2 = (red[:, k, :] for k in range(9))
                eng.wait_ge(S(f"logits{l}"), NT)
                lps = bank[7][:, 0:NT * NE].rearrange("p (t e) -> p t e", t=NT)
                link(eng.tensor_tensor(lg, lps, tiles(br[:, :]), ALU.add))
                link(eng.tensor_reduce(mx, lg, X, ALU.max))
                eng.tensor_tensor(lg, lg, over(mx, NE), ALU.subtract).then_inc(S(f"shifted{l}"), 1)
                eng.wait_ge(S(f"expd{l}"), 1)
                link(eng.tensor_reduce(sm, pr, X, ALU.add))
                link(eng.reciprocal(rs, sm))
                link(eng.tensor_tensor(pr, pr, over(rs, NE), ALU.mult))
                eng.tensor_tensor(pair[:, :, :, 0:3], prg[:, :, :, 0:3], prg[:, :, :, 1:4], ALU.add)
                eng.tensor_tensor(pair[:, :, :, 3:5], prg[:, :, :, 0:2], prg[:, :, :, 2:4], ALU.add)
                link(eng.tensor_tensor(pair[:, :, :, 5:6], prg[:, :, :, 0:1], prg[:, :, :, 3:4], ALU.add))
                link(eng.tensor_reduce(gs, pair, X, ALU.max))
                link(eng.tensor_reduce(gm, gs, X, ALU.max))
                link(eng.tensor_tensor(gk, gs, over(gm, NG), ALU.is_equal))
                link(eng.tensor_tensor(gk, gk, tiles(w4[:, :]), ALU.mult))
                link(eng.tensor_reduce(kb, gk, X, ALU.max))
                link(eng.tensor_tensor(gk, gk, over(kb, NG), ALU.is_equal))
                link(eng.tensor_scalar(gs, gk, -1.0, None, ALU.add))
                mskg = msk.rearrange("p t (g e) -> p t g e", g=NG)
                link(eng.tensor_tensor(mskg, prg, gk.unsqueeze(3).to_broadcast([P, NT, NG, EPG]), ALU.mult))
                link(eng.tensor_tensor(mskg, mskg, gs.unsqueeze(3).to_broadcast([P, NT, NG, EPG]), ALU.add))
                for v, kk, oh in ((v1, k1, oh1), (v2, k2, oh2)):
                    link(eng.tensor_reduce(v, msk, X, ALU.max))
                    link(eng.tensor_tensor(tmp, msk, over(v, NE), ALU.is_equal))
                    link(eng.tensor_tensor(tmp, tmp, tiles(w16[:, :]), ALU.mult))
                    link(eng.tensor_reduce(kk, tmp, X, ALU.max))
                    link(eng.tensor_tensor(oh, tmp, over(kk, NE), ALU.is_equal))
                    if oh is oh1:
                        link(eng.tensor_scalar(tmp, oh1, -4.0, None, ALU.mult))
                        link(eng.tensor_tensor(msk, msk, tmp, ALU.add))
                eng.tensor_tensor(asn_b[:, :], oh1.rearrange("p t e -> p (t e)"), oh2.rearrange("p t e -> p (t e)"), ALU.add).then_inc(S(f"assigned{l}"), 1)
                link(eng.tensor_tensor(sm, v1, v2, ALU.add))
                link(eng.reciprocal(rs, sm))
                eng.tensor_tensor(gates[:, :, 0], v1, rs, ALU.mult)
                link(eng.tensor_tensor(gates[:, :, 1], v2, rs, ALU.mult))
                eng.wait_ge(S(f"ranked{l}"), 1)
                eng.tensor_copy(tmp, bank[2][:, 0:NT * NE].rearrange("p (t e) -> p t e", t=NT))
                link(eng.tensor_copy(tot, bank[6][:, 0:NT * NE].rearrange("p (t e) -> p t e", t=NT)))
                for t in range(1, NT):
                    link(eng.tensor_tensor(tot[:, t, :], tot[:, t, :], tot[:, t - 1, :], ALU.add))
                link(eng.tensor_tensor(tmp[:, 1:NT, :], tmp[:, 1:NT, :], tot[:, 0:NT - 1, :], ALU.add))
                cnt = tot[:, NT - 1, :]
                link(eng.tensor_scalar(ext, cnt, float(CAP), None, ALU.is_gt))
                for m in range(2, NT):
                    link(eng.scalar_tensor_tensor(ext, cnt, float(m * CAP), ext, ALU.is_gt, ALU.add))
                link(eng.memset(dlt, 0.0))
                link(eng.tensor_tensor_scan(inc, ext, dlt, 0.0, ALU.add, ALU.add))
                link(eng.tensor_tensor(dlt, inc, ext, ALU.subtract))
                link(eng.tensor_scalar(dlt, dlt, float(CAP), float(CAP * (NE - 1)), ALU.mult, ALU.add))
                link(eng.tensor_tensor(dlt, dlt, e128[:, :], ALU.subtract))
                link(eng.tensor_scalar(slot, tmp, float(CAP), None, ALU.is_ge))
                link(eng.tensor_tensor(slot, slot, tiles(dlt), ALU.mult))
                link(eng.tensor_tensor(slot, slot, tmp, ALU.add))
                link(eng.tensor_tensor(slot, slot, tiles(e128[:, :]), ALU.add))
                link(eng.tensor_tensor(oh1, oh1, slot, ALU.mult))
                link(eng.tensor_tensor(oh2, oh2, slot, ALU.mult))
                link(eng.tensor_reduce(posf[:, :, 0], oh1, X, ALU.add))
                link(eng.tensor_reduce(posf[:, :, 1], oh2, X, ALU.add))
                link(eng.tensor_copy(pos[:, :, :], posf))
                row = cmp7[0:1]
                link(eng.tensor_tensor(row, inc[0:1].unsqueeze(1).to_broadcast([1, OVF, NE]),
                                       j7[0:1, :].unsqueeze(2).to_broadcast([1, OVF, NE]), ALU.is_le))
                link(eng.tensor_reduce(red[0:1, 9:11, :].rearrange("p a b -> p (a b)")[:, 0:OVF], row, X, ALU.add))
                ids = red[0:1, 9:11, :].rearrange("p a b -> p (a b)")
                link(eng.tensor_scalar(ids[:, 0:OVF], ids[:, 0:OVF], float(NE - 1), None, ALU.min))
                link(eng.tensor_copy(ids[:, OVF:OVF + 1], inc[0:1, NE - 1:NE]))
                eng.tensor_copy(ovf_id[0:1, :], ids).then_inc(S(f"routed{l}"), 1)
                eng.wait_ge(S(f"routed{l}"), 1)

                def evac_rows(e, b):
                    eng.wait_ge(S(f"xeT_done{l}"), e + 1)
                    eng.tensor_copy(xeT[:, b, 4:8, :], bank[1][:, :].rearrange("p (c n) -> p c n", c=4)).then_inc(S(f"xeT_dve{l}"), 1)

                def evac_hT(e, b):
                    eng.wait_ge(S(f"hT_done{l}"), e + 1)
                    eng.tensor_copy(hT[:, b, :, :], bank[4][:, 0:F].rearrange("p (c n) -> p c n", c=FC)).then_inc(S(f"hT_ready{l}"), 1)

                def times_up(e, b):
                    eng.wait_ge(S(f"silu{l}"), e + 1)
                    eng.tensor_tensor(hsb[:, b, :], ssb[:, b, :], bank[2 + b][:, F:2 * F], ALU.mult).then_inc(S(f"h_ready{l}"), 1)

                def evac_y(e, b, stored):
                    eng.wait_ge(S(f"y_done{l}"), e + 1)
                    if stored is not None:
                        eng.wait_ge(S(f"y_stored{l}{b}"), stored)
                    eng.tensor_copy(ysb[:, b, BLK:D], bank[6][:, :]).then_inc(S(f"y_dve{l}"), 1)

                def step(i, u, first=False, last=False):
                    e = 4 * i + u
                    times_up(e, u % 2)
                    if not first:
                        evac_hT(e - 1, (u - 1) % 2)
                    if not last:
                        evac_rows(e + 1, (u + 1) % 2)
                    if not first:
                        started = not isinstance(i, int) or 4 * i + u - 1 >= 2
                        evac_y(e - 1, (u - 1) % 2, 32 * i + 16 * ((u - 1) // 2) if started else None)

                evac_rows(0, 0)
                for u in range(3):
                    step(0, u, first=(u == 0))
                with eng.Fori(0, NE // 4 - 1) as i:
                    for u in range(3, 7):
                        step(i, u)
                step(NE // 4 - 1, 3, last=True)
                evac_hT(NE - 1, 1)
                evac_y(NE - 1, 1, 16 * ((NE - 1) // 2))
                n_ovf = eng.value_load(ovf_id[0:1, OVF:OVF + 1], min_val=0, max_val=OVF)
                with eng.If(n_ovf > 0):
                    eng.wait_ge(S(f"y_stored{l}0"), 16 * NE // 2)
                    with eng.Fori(0, OVF) as j:
                        eng.wait_ge(S(f"ov_turn{l}"), OV_STEPS * (j + 1) + 1)
                        eng.tensor_copy(xeT[:, 0, 4:8, :], bank[1][:, :].rearrange("p (c n) -> p c n", c=4)).then_inc(S(f"ov_turn{l}"), 1)
                        eng.wait_ge(S(f"ov_turn{l}"), OV_STEPS * (j + 1) + 5)
                        eng.tensor_tensor(hsb[:, 0, :], ssb[:, 0, :], bank[2][:, F:2 * F], ALU.mult).then_inc(S(f"ov_turn{l}"), 1)
                        eng.wait_ge(S(f"ov_turn{l}"), OV_STEPS * (j + 1) + 7)
                        eng.tensor_copy(hT[:, 0, :, :], bank[4][:, 0:F].rearrange("p (c n) -> p c n", c=FC)).then_inc(S(f"ov_turn{l}"), 1)
                        eng.wait_ge(S(f"ov_turn{l}"), OV_STEPS * (j + 1) + 9)
                        eng.tensor_copy(ysb[:, 0, BLK:D], bank[6][:, :]).then_inc(S(f"ov_turn{l}"), 1)
                for t in range(NT):
                    eng.wait_ge(S(f"gated{l}"), t + 1)
                    y1, y2 = gy[:, t % 2, 0, :], gy[:, t % 2, 1, :]
                    link(eng.scalar_tensor_tensor(y1, y2, gates[:, t, 1:2], y1, ALU.mult, ALU.add))
                    eng.scalar_tensor_tensor(xres[:, t, :], xres[:, t, :], ALPHA, y1, ALU.mult, ALU.add).then_inc(S(f"mixed{l}"), 1)
                    eng.wait_ge(S(f"mixed{l}"), t + 1)
                    norm(l, 1, t)
                    if l + 1 < DEPTH and t >= 1:
                        evac_x_tile(f"{l}1", t - 1)
                if l + 1 < DEPTH:
                    evac_x_tile(f"{l}1", NT - 1)


_INS = ["x", "ln_gain", "ln_bias", "swa_w_in", "swa_sinks", "swa_w_o", "fox_w_in", "fox_b_f", "fox_w_o",
        "w_router", "b_router", "w_gate", "w_up", "w_down"]


def kernel(**inputs):
    import numpy as np
    import concourse.bacc as bacc
    from concourse.bass_utils import run_bass_kernel_spmd

    half = ROT // 2
    inv_freq = np.power(np.float32(500000.0), -np.arange(half, dtype=np.float32) * np.float32(2.0 / ROT)).astype(np.float32)
    ang = np.arange(SEQ, dtype=np.float32)[:, None] * inv_freq[None, :]
    rope = np.stack([np.tile(np.cos(ang), 2), np.tile(np.sin(ang), 2)], axis=1).astype(np.float32)

    nc = bacc.Bacc("TRN2", target_bir_lowering=False, num_devices=1)
    arrays, args = {}, []
    for name in _INS:
        a = np.ascontiguousarray(inputs[name])
        arrays[f"in_{name}"] = a
        args.append(nc.dram_tensor(f"in_{name}", a.shape, mybir.dt.from_np(a.dtype), kind="ExternalInput").ap())
    arrays["rope"] = rope
    args.append(nc.dram_tensor("rope", rope.shape, mybir.dt.float32, kind="ExternalInput").ap())
    args.append(nc.dram_tensor("out", (1, SEQ, D), mybir.dt.float32, kind="ExternalOutput").ap())
    trunk(nc, *args)
    r = run_bass_kernel_spmd(nc, [arrays], core_ids=[0])
    return r.results[0]["out"]
```

```python
import concourse.bass as bass
from concourse import mybir
from contextlib import ExitStack

P = 128
SEQ, D = 512, 1024
HD = 64
NH = D // HD
NKV = NH // 4
WINDOW = 128
NT = SEQ // P
KC = D // P
BLK = 512
NE, NG, TOPK = 16, 4, 2
EPG = NE // NG
F = D // 4
FC = F // P
ROT = HD // 4
DEPTH = 2
ALPHA = (2.0 * DEPTH) ** 0.25
LN_EPS = 1e-5
SCALE = HD ** -0.5
NEG = -1e30
CAP = 96
OVF = (SEQ * TOPK - 1) // CAP
SLOTS = (NE + OVF) * CAP
PAIRS = NH // 2
UNITS = NH * NT
RING = 4
SLOT_WORDS = KC * BLK + FC * D
IN_BLOCKS = (3, 6)
OUT_BLOCKS = 2
IN_USE = (0, IN_BLOCKS[0] + OUT_BLOCKS + NE)
OUT_USE = tuple(IN_USE[l] + IN_BLOCKS[l] for l in range(DEPTH))
IN_ORDER = ((0, 1, 2), (4, 5, 0, 1, 2, 3))
EXP_USE = tuple(OUT_USE[l] + OUT_BLOCKS for l in range(DEPTH))


def trunk(nc, x, ln_gain, ln_bias, swa_w_in, swa_sinks, swa_w_o, fox_w_in, fox_b_f, fox_w_o,
          w_router, b_router, w_gate, w_up, w_down, rope, out):
    fp32, fp32r, bf16, i32, u32 = mybir.dt.float32, mybir.dt.float32r, mybir.dt.bfloat16, mybir.dt.int32, mybir.dt.uint32
    ALU = mybir.AluOpType
    ACT = mybir.ActivationFunctionType
    X = mybir.AxisListType.X

    ctx = ExitStack()
    with ctx:
        def sb(name, shape, dt=fp32):
            return ctx.enter_context(nc.sbuf_tensor(name, shape, dt))

        base = -(-nc.sbuf_base // 32) * 32
        xres = sb("xres", [P, NT, D])
        xT = sb("xT", [P, KC, SEQ])
        ring = sb("ring", [P, RING, SLOT_WORDS])
        lnp = sb("lnp", [P, 2, D])
        ident = sb("ident", [P, P])
        before_b = sb("before_b", [P, P], bf16)
        ones_b = sb("ones_b", [P, P], bf16)
        asn_b = sb("asn_b", [P, NT * NE], bf16)
        band = sb("band", [P, 2, P])
        causal_b = sb("causal_b", [P, SEQ], bf16)
        ident_b = sb("ident_b", [P, P], bf16)
        cs = sb("cs", [P, NT, 2, ROT])
        sink = sb("sink", [P, NH])
        wr = sb("wr", [P, KC, NE])
        wf = sb("wf", [P, KC, NH])
        br = sb("br", [P, NE])
        bf = sb("bf", [NH, 1])
        stats = sb("stats", [P, NT, 2, 6])
        mv = sb("mv", [P, NT, 2])
        veps = sb("veps", [P, NT])
        rstd = sb("rstd", [P, NT])
        mhalf = sb("mhalf", [P, NT])
        nmax = sb("nmax", [P, 8])
        rsum = sb("rsum", [P, 8])
        rinv = sb("rinv", [P, 8])
        gates = sb("gates", [P, NT, 2])
        pos = sb("pos", [P, NT, 2], u32)
        ovf_id = sb("ovf_id", [1, OVF + 1], i32)
        arena_at = -(-nc.sbuf_base // 32) * 32
        arena = sb("arena", [P, 12288 + KC * SEQ + 2 * KC * NH])

        def area(at, n, pattern=None, **kw):
            a = arena[:, at:at + n]
            return a.rearrange(pattern, **kw) if pattern else a

        QT = area(0, PAIRS * SEQ, "p (h t) -> p h t", h=PAIRS)
        KT = area(4096, PAIRS * SEQ, "p (h t) -> p h t", h=PAIRS)
        V = area(8192, NT * D, "p (t n) -> p t n", t=NT)
        sp = area(12288, 4 * 516, "p (b n) -> p b n", b=4)
        pT = area(14352, 2 * SEQ, "p (b n) -> p b n", b=2)
        rtmp = area(15376, 2 * 8 * ROT, "p (a n) -> p a n", a=2)
        tok = area(6144, 2 * BLK, "p (b n) -> p b n", b=2)
        V0 = area(7168, NT * F, "p (t n) -> p t n", t=NT)
        zeros = area(14352, D)
        ones, before = area(14352, P), area(14352 + P, P)
        cb = lnp[:, :, :].rearrange("p b (h n) -> p b h n", h=2)
        fz = area(4096, 4 * SEQ, "p (k n) -> p k n", k=4)
        def small(at, *shape):
            n = 1
            for s in shape:
                n *= s
            a = area(at, n)
            if len(shape) == 2:
                return a.rearrange("p (a b) -> p a b", a=shape[0])
            if len(shape) == 3:
                return a.rearrange("p (a b c) -> p a b c", a=shape[0], b=shape[1])
            return a
        lg, pr, tmp, msk, oh1, oh2, tot, slot = (small(14000 + 64 * k, NT, NE) for k in range(8))
        prg = area(14064, 64).rearrange("p (t g e) -> p t g e", t=NT, g=NG)
        pair = small(14512, NT, NG, 6)
        gs, gk = small(14608, NT, NG), small(14624, NT, NG)
        red = small(14640, 10, NT)
        ids = small(14684, OVF + 1)
        ext, inc, dlt = (small(14704 + 16 * k, NE) for k in range(3))
        posf = small(14800, NT, 2)
        cmpo = small(14840, OVF, NE)
        picks = area(9728, NT * CAP, "p (t n) -> p t n", t=NT)
        w4 = sb("w4", [P, NG])
        w16 = sb("w16", [P, NE])
        e_cap = sb("e_cap", [P, NE])
        jo = sb("jo", [P, OVF])
        places = sb("places", [P, CAP])
        xe = area(0, 4 * D, "p (b n) -> p b n", b=4)
        xeT = area(4096, 2 * KC * CAP, "p (b c n) -> p b c n", b=2, c=KC)
        ssb = area(6144, 2 * F, "p (b n) -> p b n", b=2)
        hsb = area(6656, 2 * F, "p (b n) -> p b n", b=2)
        hT = area(7168, 2 * FC * CAP, "p (b c n) -> p b c n", b=2, c=FC)
        ysb = area(7680, 2 * D, "p (b n) -> p b n", b=2)
        gy = area(0, 4 * D, "p (b k n) -> p b k n", b=2, k=2)

        xT_at = base + 4 * NT * D
        ring_at = xT_at + 4 * KC * SEQ

        attn_high = nc.alloc_sbuf_tensor_at("attn_high", [P, KC, SEQ], fp32r, offset=xT_at)
        attn_low = nc.alloc_sbuf_tensor_at("attn_low", [P, KC, SEQ], fp32r, offset=arena_at)

        def behind_block(name, slot, shape):
            return nc.alloc_sbuf_tensor_at(name, shape, fp32r, offset=ring_at + 4 * (slot * SLOT_WORDS + KC * BLK))
        xlow = nc.alloc_sbuf_tensor_at("xlow", [P, KC, SEQ], fp32r, offset=xT_at)
        x1_high = nc.alloc_sbuf_tensor_at("x1_high", [P, KC, SEQ], fp32r, offset=arena_at + 4 * 12288)
        wf_parts = nc.alloc_sbuf_tensor_at("wf_parts", [P, 2, KC, NH], fp32r, offset=arena_at + 4 * (12288 + KC * SEQ))
        x0_high = nc.alloc_sbuf_tensor_at("x0_high", [P, KC, SEQ], fp32r, offset=arena_at + 4 * 8192)
        halves = [behind_block(f"high{i}", i, [P, KC // 2, BLK]) for i in range(RING)]
        lows = [nc.alloc_sbuf_tensor_at(f"low{i}", [P, KC, BLK], fp32r, offset=ring_at + 4 * i * SLOT_WORDS) for i in range(RING)]

        def split(use, pair, c):
            return slot_in(use)[:, c, :], halves[2 * pair + c // 4][:, c % 4, :], lows[use % RING][:, c, :]

        wsplit = [behind_block(f"wsplit{i}", i, [P, 2, KC, P]) for i in range(2)]

        bank = [ctx.enter_context(nc.psum_tensor(f"bank{i}", [P, 512], fp32)) for i in range(8)]

        xs = nc.dram_tensor("xs", [SLOTS, D], fp32).ap()
        ys = nc.dram_tensor("ys", [SLOTS, D], fp32).ap()
        cd = nc.dram_tensor("cd", [NH, SEQ], fp32).ap()
        xs_t = xs.rearrange("(e p) d -> e p d", p=CAP)
        ys_t = ys.rearrange("(e p) d -> e p d", p=CAP)

        sems = {}

        def S(name):
            if name not in sems:
                sems[name] = ctx.enter_context(nc.semaphore(name))
            return sems[name]

        def chain(eng, name):
            n = [0]

            def link(ins):
                n[0] += 1
                ins.then_inc(S(name), 1)
                eng.wait_ge(S(name), n[0])
            return link

        def slot_in(k):
            return ring[:, k % RING, 0:KC * BLK].rearrange("p (c n) -> p c n", c=KC)

        def slot_down(k):
            return ring[:, k % RING, KC * BLK:SLOT_WORDS].rearrange("p (c n) -> p c n", c=FC)

        def weights_here(eng, k, more=0):
            eng.wait_ge(S(f"w_loaded{k % RING}"), ring_count(k) + more)

        def n_dmas(k):
            return 3 if any(EXP_USE[l] <= k < EXP_USE[l] + NE for l in range(DEPTH)) else 1

        def ring_count(k):
            return 16 * sum(n_dmas(j) for j in range(k % RING, k + 1, RING))

        OV_STEPS = 11
        UNIT = [(hp, n, half) for hp in range(PAIRS) for n in (0, 3, 1, 2) for half in range(2)]
        GROUPS = (IN_BLOCKS[0] * NT, 4 * 4 + 2 * NT)

        def s_bank(u):
            return bank[(0, 1, 2, 7)[u % 4]]

        block = ctx.enter_context(nc.Block())

        @block.sync
        def _(eng):
            def load_x(t):
                eng.dma_start(xres[:, t, :], x[0, t * P:(t + 1) * P, :]).then_inc(S(f"x_in{t}"), 16)

            load_x(0)
            def wait_used(k):
                l = 0 if k < IN_USE[1] else 1
                if k < OUT_USE[l]:
                    j = k - IN_USE[l]
                    eng.wait_ge(S(f"proj_done{l}"), 4 * (j + 1) if l == 0 else max(2 * NT, 4 * (j + 1)))
                elif k < EXP_USE[l]:
                    eng.wait_ge(S(f"wo_done{l}"), OUT_BLOCKS * (NT - 1) + k - OUT_USE[l] + 1)
                else:
                    eng.wait_ge(S(f"y_done{l}"), k - EXP_USE[l] + 1)

            def load_block(k, src):
                if k >= RING:
                    wait_used(k - RING)
                eng.dma_start(slot_in(k), src.rearrange("(c p) n -> p c n", p=P)).then_inc(S(f"w_loaded{k % RING}"), 16)

            def load_expert(s, w, e, sem):
                load_gate_up(s, w, e, sem)
                load_down(s, w, e, sem)

            def load_gate_up(s, w, e, sem):
                gu = slot_in(s)
                eng.dma_start(gu[:, :, 0:F], w_gate[w, e].rearrange("(c p) f -> p c f", p=P)).then_inc(sem, 16)
                eng.dma_start(gu[:, :, F:2 * F], w_up[w, e].rearrange("(c p) f -> p c f", p=P)).then_inc(sem, 16)

            def load_down(s, w, e, sem):
                eng.dma_start(slot_down(s), w_down[w, e].rearrange("(c p) n -> p c n", p=P)).then_inc(sem, 16)

            for l, (w_in, w_o) in enumerate(((swa_w_in[0], swa_w_o[0]), (fox_w_in[0], fox_w_o[0]))):
                for j in range(IN_BLOCKS[l]):
                    c = IN_ORDER[l][j]
                    if l == 1 and j == 2:
                        for b in range(2):
                            eng.wait_ge(S(f"gy_in0{b}"), 64)
                    load_block(IN_USE[l] + j, w_in[:, BLK * c:BLK * (c + 1)])
                    if l == 0 and j == 0:
                        load_x(1)
                        eng.dma_start(cs[:, :, :, :], rope.rearrange("(t p) a n -> p t a n", p=P)).then_inc(S("const_in"), 16)
                        eng.dma_start(sink[:, :], swa_sinks[0].partition_broadcast(P)).then_inc(S("const_in"), 16)
                        eng.dma_start(wr[:, :, :], w_router.rearrange("(c p) n -> p c n", p=P)).then_inc(S("const_in"), 16)
                        eng.dma_start(br[:, :], b_router.partition_broadcast(P)).then_inc(S("const_in"), 16)
                        eng.dma_start(bf[:, :], fox_b_f.rearrange("a h -> h a")).then_inc(S("const_in"), 16)
                        eng.dma_start(wf[:, :, :], fox_w_in[0][:, 3 * D:3 * D + NH].rearrange("(c p) n -> p c n", p=P)).then_inc(S("const_in"), 16)
                        load_x(2)
                        load_x(3)
                for j in range(OUT_BLOCKS):
                    load_block(OUT_USE[l] + j, w_o[:, BLK * j:BLK * (j + 1)])
                for u in range(OUT_BLOCKS):
                    k = EXP_USE[l] + u
                    wait_used(k - RING)
                    load_gate_up(k, l, u, S(f"w_loaded{k % RING}"))
                eng.wait_ge(S(f"wo_done{l}"), OUT_BLOCKS * NT)
                for u in range(RING):
                    k = EXP_USE[l] + u
                    if u >= OUT_BLOCKS:
                        load_gate_up(k, l, u, S(f"w_loaded{k % RING}"))
                    load_down(k, l, u, S(f"w_loaded{k % RING}"))
                with eng.Fori(1, NE // RING) as i:
                    for u in range(RING):
                        k = EXP_USE[l] + u
                        eng.wait_ge(S(f"y_done{l}"), RING * i + u - (RING - 1))
                        load_expert(k, l, RING * i + u, S(f"w_loaded{k % RING}"))
                eng.wait_ge(S(f"routed{l}"), 1)
                n_ovf = eng.value_load(ovf_id[0:1, OVF:OVF + 1], min_val=0, max_val=OVF)
                k = EXP_USE[l] + NE
                with eng.If(n_ovf > 0):
                    wait_used(k - RING)
                    with eng.Fori(0, OVF) as j:
                        e = eng.value_load(ovf_id[0:1, bass.ds(j, 1)], min_val=0, max_val=NE - 1)
                        eng.wait_ge(S(f"ov_turn{l}"), OV_STEPS * (j + 1))
                        load_expert(k, l, e, S(f"ov_in{l}"))
                        eng.dma_start(xe[0:CAP, 0, :], xs_t[j + NE]).then_inc(S(f"ov_in{l}"), 16)
                        eng.wait_ge(S(f"ov_turn{l}"), OV_STEPS * (j + 1) + 11)
                        eng.dma_start(ys_t[j + NE], ysb[0:CAP, 0, :]).then_inc(S(f"ov_stored{l}"), 16)
            for t in range(NT):
                eng.wait_ge(S(f"x_ready{l}1"), t + 1)
                eng.dma_start(out[0, t * P:(t + 1) * P, :], xres[:, t, :]).then_inc(S("out_done"), 16)
            eng.wait_ge(S("out_done"), 16 * NT)

        @block.gpsimd
        def _(eng):
            link = chain(eng, "pool_step")
            link(eng.memset(ident[:, :], 0.0))
            eng.affine_select(out=ident[:, :], in_=ident[:, :], compare_op=ALU.not_equal, fill=1.0,
                              base=0, pattern=[[-1, P]], channel_multiplier=1).then_inc(S("ident"), 1)
            eng.wait_ge(S("ident"), 1)
            link(eng.memset(ones, 1.0))
            link(eng.affine_select(out=before, in_=ones, compare_op=ALU.is_ge, fill=0.0,
                                   base=-1, pattern=[[1, P]], channel_multiplier=-1))
            link(eng.memset(band[:, :, :], 0.0))
            link(eng.memset(causal_b[:, :], 0.0))
            link(eng.affine_select(out=band[:, 0, :], in_=band[:, 0, :], compare_op=ALU.is_ge, fill=NEG / SCALE,
                                   base=-1, pattern=[[1, P]], channel_multiplier=-1))
            link(eng.affine_select(out=band[:, 1, :], in_=band[:, 1, :], compare_op=ALU.is_ge, fill=NEG / SCALE,
                                   base=0, pattern=[[-1, P]], channel_multiplier=1))
            link(eng.iota(w4[:, :], [[-1, NG]], base=NG, channel_multiplier=0, allow_small_or_imprecise_dtypes=True))
            link(eng.iota(w16[:, :], [[-1, NE]], base=NE, channel_multiplier=0, allow_small_or_imprecise_dtypes=True))
            link(eng.iota(e_cap[:, :], [[CAP, NE]], base=0, channel_multiplier=0, allow_small_or_imprecise_dtypes=True))
            link(eng.iota(jo[:, :], [[1, OVF]], base=0, channel_multiplier=0, allow_small_or_imprecise_dtypes=True))
            link(eng.iota(places[:, :], [[1, CAP]], base=0, channel_multiplier=0, allow_small_or_imprecise_dtypes=True))
            link(eng.memset(mhalf[:, :], -0.5))
            link(eng.tensor_copy(before_b[:, :], before))
            link(eng.tensor_copy(ones_b[:, :], ones))
            link(eng.tensor_copy(ident_b[:, :], ident[:, :]))
            link(eng.tensor_copy(causal_b[:, SEQ - P:SEQ], band[:, 1, :]))
            eng.memset(zeros, 0.0).then_inc(S("consts"), 1)
            eng.wait_ge(S("consts"), 1)
            eng.wait_ge(S(f"w_loaded{2}"), 16)
            eng.dma_start(xs.rearrange("(e p) d -> p e d", p=CAP),
                          zeros[0:CAP].unsqueeze(1).to_broadcast([CAP, NE + OVF, D])).then_inc(S("cleared"), 16)
            eng.dma_start(ys.rearrange("(e p) d -> p e d", p=CAP)[:, NE:NE + OVF, :],
                          zeros[0:CAP].unsqueeze(1).to_broadcast([CAP, OVF, D])).then_inc(S("cleared"), 16)
            eng.wait_ge(S("cleared"), 32)
            eng.drain().then_inc(S("zeros_free"), 1)

            def load_norm(l, w):
                eng.dma_start(lnp[:, 0, :], ln_gain[l, w].partition_broadcast(P)).then_inc(S("ln_in"), 16)
                eng.dma_start(lnp[:, 1, :], ln_bias[l, w].partition_broadcast(P)).then_inc(S("ln_in"), 16)

            def norm_rstd(l, w, gather=None):
                for t in range(NT):
                    eng.wait_ge(S(f"ln_stats{l}{w}"), t + 1)
                    link(eng.tensor_scalar(veps[:, t:t + 1], mv[:, t, 1:2], LN_EPS, None, ALU.add))
                    eng.tensor_tensor(rstd[:, t:t + 1], veps[:, t:t + 1], mhalf[:, t:t + 1], ALU.pow).then_inc(S(f"rstd{l}{w}"), 1)
                    if gather and t + 2 < NT:
                        gather(t + 2)
                if w == 0:
                    eng.wait_ge(S(f"x_ready{l}{w}"), NT)
                    load_norm(l, 1)

            def load_bias(hp):
                eng.dma_start(cb[:, hp % 2, :, :], cd[2 * hp:2 * hp + 2].partition_broadcast(P)).then_inc(S(f"cb_in{hp % 2}"), 16)

            load_norm(0, 0)
            for l in range(DEPTH):
                if l == 1:
                    eng.wait_ge(S("decay"), 1)
                    eng.dma_start(cd, fz[0:NH, 3, :]).then_inc(S("cd_out"), 16)
                    eng.wait_ge(S("cd_out"), 16)
                    eng.wait_ge(S("x_ready01"), NT)
                    load_bias(0)
                    load_bias(1)
                for hp in range(PAIRS):
                    for p in range(2 * hp, 2 * hp + 2):
                        w, high, low = split(OUT_USE[l] + p // KC, p // KC, p % KC)
                        eng.wait_ge(S(f"out_high{l}"), p + 1)
                        eng.tensor_tensor(low, w, high, ALU.subtract).then_inc(S(f"out_low{l}"), 1)
                    if l == 1 and hp + 2 < PAIRS:
                        eng.wait_ge(S(f"sp_ready{l}"), 2 * NT * (hp + 1))
                        load_bias(hp + 2)
                if l == 1:
                    eng.wait_ge(S(f"sp_ready{l}"), UNITS)
                    load_norm(1, 0)
                norm_rstd(l, 0)
                eng.wait_ge(S("placed"), l + 1)
                for t in range(NT):
                    for k in range(TOPK):
                        eng.indirect_dma_start(xs, bass.IndirectOffsetOnAxis(ap=pos[:, t, k:k + 1], axis=0),
                                               xres[:, t, :], None).then_inc(S(f"scattered{l}"), 16)
                for b in range(2):
                    eng.wait_ge(S(f"y_stored{l}{b}"), 16 * NE // 2)
                n_ovf = eng.value_load(ovf_id[0:1, OVF:OVF + 1], min_val=0, max_val=OVF)
                with eng.If(n_ovf > 0):
                    eng.sem_inc(S(f"ov_turn{l}"), OV_STEPS)
                    with eng.Fori(0, OVF) as j:
                        eng.wait_ge(S(f"ov_stored{l}"), 16 * j + 16)
                def gather(t):
                    if t >= 2:
                        eng.wait_ge(S(f"mixed{l}"), t - 1)
                    for k in range(TOPK):
                        eng.indirect_dma_start(gy[:, t % 2, k, :], None, ys,
                                               bass.IndirectOffsetOnAxis(ap=pos[:, t, k:k + 1], axis=0)).then_inc(S(f"gy_in{l}{t % 2}"), 16)
                gather(0)
                gather(1)
                norm_rstd(l, 1, gather)

        @block.tensor
        def _(eng):
            def turn_x(t, a):
                if a == "in":
                    eng.wait_ge(S(f"x_in{t}"), 16)
                else:
                    eng.wait_ge(S(f"x_ready{a}"), t + 1)
                if t >= 1:
                    eng.wait_ge(S(f"xt_act{a}"), t)
                    eng.wait_ge(S(f"xt_dve{a}"), t)
                for c in range(KC):
                    mm = eng.transpose(bank[3 + c // 4][:, (c % 4) * P:(c % 4 + 1) * P],
                                       xres[:, t, c * P:(c + 1) * P], ident[:, :])
                mm.then_inc(S(f"xt_done{a}"), 1)

            eng.wait_ge(S("ident"), 1)
            turn_x(0, "in")
            for l in range(DEPTH):
                def xT_here(a, t):
                    eng.wait_ge(S(f"xt_act{a}"), t + 1)
                    eng.wait_ge(S(f"xt_dve{a}"), t + 1)

                def three(out, ah, al, wh, wl, c):
                    eng.matmul(out, ah, wh, start=(c == 0), stop=False)
                    eng.matmul(out, ah, wl, start=False, stop=False)
                    return eng.matmul(out, al, wh, start=False, stop=(c == KC - 1))

                if l == 0:
                    def turn_heads(k):
                        eng.wait_ge(S("roped"), k + 1)
                        if k >= 2:
                            eng.wait_ge(S("qkT_free"), k - 1)
                        for i in range(4):
                            mm = eng.transpose(bank[5 + k % 2][:, i * P:(i + 1) * P], tok[:, k % 2, i * P:(i + 1) * P], ident[:, :])
                        mm.then_inc(S("qkT_done"), 1)

                    for j in range(IN_BLOCKS[0]):
                        for t in range(NT):
                            k = NT * j + t
                            xT_here("in", t)
                            if k >= 2:
                                eng.wait_ge(S(f"proj_free{l}{k % 2}"), k // 2)
                            for c in range(KC):
                                if k < NT - 1 and c == KC // 2:
                                    turn_x(t + 1, "in")
                                if t == 0:
                                    eng.wait_ge(S("in_low"), KC * j + c + 1)
                                _, wh, wl = split(j, j % 2, c)
                                cols = slice(t * P, (t + 1) * P)
                                mm = three(bank[k % 2][:, :], x0_high[:, c, cols], xlow[:, c, cols], wh, wl, c)
                            mm.then_inc(S(f"proj_done{l}"), 1)
                            if k >= 1:
                                turn_heads(k - 1)
                    turn_heads(GROUPS[0] - 1)
                    eng.wait_ge(S("qkT_free"), GROUPS[0])
                else:
                    turn_x(0, "01")
                    for t in range(NT):
                        xT_here("01", t)
                        cols = slice(t * P, (t + 1) * P)
                        for b in range(2):
                            k = 2 * t + b
                            if b == 1 and 1 <= t < NT - 1:
                                turn_x(t + 1, "01")
                            if t == 0:
                                eng.wait_ge(S("v_low"), KC * (b + 1))
                            else:
                                eng.wait_ge(S(f"proj_free{l}{b}"), t)
                            for c in range(KC):
                                _, wh, wl = split(IN_USE[1] + b, b, c)
                                mm = three(bank[b][:, :], x1_high[:, c, cols], xlow[:, c, cols], wh, wl, c)
                            mm.then_inc(S(f"proj_done{l}"), 1)
                        if t == 0:
                            turn_x(1, "01")
                    eng.wait_ge(S("wf_low"), 1)
                    for c in range(KC):
                        mm = three(bank[7][0:NH, :], wf_parts[:, 0, c, :], wf_parts[:, 1, c, :], x1_high[:, c, :], xlow[:, c, :], c)
                    mm.then_inc(S("forget"), 1)
                    for g in range(4 * 4):
                        k = 2 * NT + g
                        eng.wait_ge(S(f"proj_free{l}{k % 2}"), k // 2)
                        eng.wait_ge(S("w_high"), g + 1)
                        eng.wait_ge(S("w_low"), g + 1)
                        for c in range(KC):
                            xh, xl = x1_high[:, c, :], xlow[:, c, :]
                            wh, wl = wsplit[g % 2][:, 0, c, :], wsplit[g % 2][:, 1, c, :]
                            mm = three(bank[k % 2][:, :], wh, wl, xh, xl, c)
                        mm.then_inc(S(f"proj_done{l}"), 1)
                    for b in range(2):
                        eng.wait_ge(S(f"proj_free{l}{b}"), GROUPS[1] // 2)

                def keys(n):
                    return (max(n - 1, 0), n + 1) if l == 0 else (0, n + 1)

                def scores(u):
                    hp, n, half = UNIT[u]
                    k0, k1 = keys(n)
                    if u >= 4:
                        eng.wait_ge(S(f"sp_ready{l}"), u - 3)
                    r = slice(HD * half, HD * half + HD)
                    kp = (2 * hp + half) // (NH // NKV) if l == 0 else hp
                    nk = (k1 - k0) * P
                    if l == 1:
                        eng.matmul(s_bank(u)[:, 0:nk], ident_b[:, :], causal_b[:, SEQ - nk:SEQ], start=True, stop=False)
                    eng.matmul(s_bank(u)[:, 0:nk], QT[r, hp, n * P:(n + 1) * P], KT[r, kp, k0 * P:k1 * P],
                               start=(l == 0), stop=True).then_inc(S(f"s_done{l}"), 1)

                def turn_probs(u):
                    hp, n, half = UNIT[u]
                    k0, k1 = keys(n)
                    eng.wait_ge(S(f"p_ready{l}"), u + 1)
                    if u >= 2:
                        eng.wait_ge(S(f"pT_ready{l}{half}"), u // 2)
                    for i in range(k1 - k0):
                        mm = eng.transpose(bank[3 + u % 2][:, i * P:(i + 1) * P], sp[:, u % 4, i * P:(i + 1) * P], ident[:, :])
                    mm.then_inc(S(f"pT_done{l}"), 1)

                def mix(u):
                    hp, n, half = UNIT[u]
                    k0, k1 = keys(n)
                    k = u // 2
                    eng.wait_ge(S(f"pT_ready{l}{half}"), k + 1)
                    if k >= 2 and half == 0:
                        eng.wait_ge(S(f"aT_ready{l}"), k - 1)
                    v = HD * ((2 * hp + half) // (NH // NKV) if l == 0 else 2 * hp + half)
                    for i in range(k1 - k0):
                        mm = eng.matmul(bank[5 + k % 2][HD * half:HD * half + HD, 0:P], (V0 if l == 0 else V)[:, k0 + i, v:v + HD],
                                        pT[:, u % 2, i * P:(i + 1) * P], start=(i == 0), stop=(i == k1 - k0 - 1))
                    mm.then_inc(S(f"pv_done{l}"), 1)

                if l == 0:
                    eng.wait_ge(S("consts"), 1)
                for u in range(3):
                    scores(u)
                for u in range(UNITS):
                    if u + 3 < UNITS:
                        scores(u + 3)
                    turn_probs(u)
                    if u >= 1:
                        mix(u - 1)
                mix(UNITS - 1)

                def route(t):
                    xT_here(f"{l}0", t)
                    if t == 0:
                        eng.wait_ge(S("const_in"), 96)
                    for c in range(KC):
                        mm = eng.matmul(bank[7][:, t * NE:(t + 1) * NE], xT[:, c, t * P:(t + 1) * P], wr[:, c, :],
                                        start=(c == 0), stop=(c == KC - 1))
                    mm.then_inc(S(f"logits{l}"), 1)

                eng.wait_ge(S(f"aT_ready{l}"), UNITS // 2)
                for t in range(NT):
                    for b in range(OUT_BLOCKS):
                        g = OUT_BLOCKS * t + b
                        if g >= 2:
                            eng.wait_ge(S(f"res_done{l}"), g - 1)
                        if t == 0:
                            eng.wait_ge(S(f"out_low{l}"), KC * (b + 1))
                        for c in range(KC):
                            ah, al = (a[:, c, t * P:(t + 1) * P] for a in (attn_high, attn_low))
                            _, wh, wl = split(OUT_USE[l] + b, b, c)
                            mm = three(bank[b][:, :], ah, al, wh, wl, c)
                        mm.then_inc(S(f"wo_done{l}"), 1)
                        if t >= 1 and b == 0:
                            turn_x(t - 1, f"{l}0")
                    if t >= 1:
                        route(t - 1)
                turn_x(NT - 1, f"{l}0")
                route(NT - 1)
                eng.wait_ge(S("assigned"), l + 1)
                eng.matmul(bank[2][:, 0:NT * NE], before_b[:, :], asn_b[:, :], start=True, stop=True)
                eng.matmul(bank[6][:, 0:NT * NE], ones_b[:, :], asn_b[:, :], start=True, stop=True).then_inc(S("ranked"), 1)

                def turn_rows(b):
                    for c in range(KC):
                        mm = eng.transpose(bank[c // 4][:, (c % 4) * P:(c % 4) * P + CAP], xe[0:CAP, b, c * P:(c + 1) * P], ident[0:CAP, 0:CAP])
                    return mm

                def gate_up(b, use):
                    w = slot_in(use)
                    for c in range(KC):
                        mm = eng.matmul(bank[2 + b][0:CAP, :], xeT[:, b, c, :], w[:, c, :], start=(c == 0), stop=(c == KC - 1))
                    return mm

                def turn_h(b):
                    for c in range(FC):
                        mm = eng.transpose(bank[4][:, c * P:c * P + CAP], hsb[0:CAP, b, c * P:(c + 1) * P], ident[0:CAP, 0:CAP])
                    return mm

                def down(b, use):
                    w = slot_down(use)
                    for half in range(2):
                        for c in range(FC):
                            mm = eng.matmul(bank[5 + half][0:CAP, :], hT[:, b, c, :], w[:, c, half * BLK:(half + 1) * BLK],
                                            start=(c == 0), stop=(c == FC - 1))
                    return mm

                def step(i, u, first=False, last=False):
                    use = EXP_USE[l] + u
                    e = 4 * i + u
                    eng.wait_ge(S(f"xeT_act{l}"), e + 1)
                    eng.wait_ge(S(f"xeT_dve{l}"), e + 1)
                    eng.wait_ge(S(f"w_loaded{use % RING}"), 48 * i + ring_count(use))
                    gate_up(u % 2, use).then_inc(S(f"gu_done{l}"), 1)
                    if not first:
                        eng.wait_ge(S(f"h_ready{l}"), e)
                        turn_h((u - 1) % 2).then_inc(S(f"hT_done{l}"), 1)
                    if not last:
                        eng.wait_ge(S(f"xe_in{l}{(u + 1) % 4}"), 16 * i + 16 * ((u + 1) // 4) + (16 if (u + 1) % 4 else 0))
                        turn_rows((u + 1) % 4).then_inc(S(f"xeT_done{l}"), 1)
                    if not first:
                        down_of(e - 1, (u - 1) % 2, use - 1, u > 1 or not isinstance(i, int) or i > 0)

                def down_of(e, b, use, reused):
                    eng.wait_ge(S(f"hT_ready{l}"), e + 1)
                    if reused:
                        eng.wait_ge(S(f"y_act{l}"), e)
                        eng.wait_ge(S(f"y_dve{l}"), e)
                    down(b, use).then_inc(S(f"y_done{l}"), 1)

                eng.wait_ge(S("picks_ready"), l + 1)
                for half in range(2):
                    for t in range(NT):
                        mm = eng.matmul(bank[half][0:CAP, :], picks[:, t, :], xres[:, t, half * BLK:(half + 1) * BLK],
                                        start=(t == 0), stop=(t == NT - 1))
                    mm.then_inc(S(f"picked{l}"), 1)
                eng.wait_ge(S(f"xe0_ready{l}"), 2)
                turn_rows(0).then_inc(S(f"xeT_done{l}"), 1)
                step(0, 0, first=True)
                step(0, 1)
                with eng.Fori(0, NE // 4 - 1) as i:
                    for u in range(2, 6):
                        step(i, u)
                for u in range(2, 4):
                    step(NE // 4 - 1, u, last=(u == 3))
                eng.wait_ge(S(f"h_ready{l}"), NE)
                turn_h(1).then_inc(S(f"hT_done{l}"), 1)
                down_of(NE - 1, 1, EXP_USE[l] + NE - 1, True)
                n_ovf = eng.value_load(ovf_id[0:1, OVF:OVF + 1], min_val=0, max_val=OVF)
                with eng.If(n_ovf > 0):
                    eng.wait_ge(S(f"y_act{l}"), NE)
                    eng.wait_ge(S(f"y_dve{l}"), NE)
                    with eng.Fori(0, OVF) as j:
                        eng.wait_ge(S(f"ov_in{l}"), 64 * j + 64)
                        turn_rows(0).then_inc(S(f"ov_turn{l}"), 1)
                        eng.wait_ge(S(f"ov_turn{l}"), OV_STEPS * (j + 1) + 3)
                        gate_up(0, EXP_USE[l] + NE).then_inc(S(f"ov_turn{l}"), 1)
                        eng.wait_ge(S(f"ov_turn{l}"), OV_STEPS * (j + 1) + 6)
                        turn_h(0).then_inc(S(f"ov_turn{l}"), 1)
                        eng.wait_ge(S(f"ov_turn{l}"), OV_STEPS * (j + 1) + 8)
                        down(0, EXP_USE[l] + NE).then_inc(S(f"ov_turn{l}"), 1)

        @block.scalar
        def _(eng):
            def evac_x(a, t):
                eng.wait_ge(S(f"xt_done{a}"), t + 1)
                eng.copy(xT[:, 0:4, t * P:(t + 1) * P], bank[3][:, :].rearrange("p (c n) -> p c n", c=4)).then_inc(S(f"xt_act{a}"), 1)

            def high_weights(g):
                use = IN_USE[1] + 2 + g // 4
                weights_here(eng, use)
                eng.wait_ge(S("proj_done1"), 2 * NT + g - 1 if g >= 2 else 2 * NT - 1)
                eng.copy(wsplit[g % 2][:, 0, :, :], slot_in(use)[:, :, (g % 4) * P:(g % 4 + 1) * P]).then_inc(S("w_high"), 1)

            def in_weights_high(p):
                j = p // KC
                w, high, _ = split(j, j % 2, p % KC)
                weights_here(eng, j)
                if j >= 2:
                    eng.wait_ge(S("proj_done0"), NT * (j - 1))
                eng.copy(high, w).then_inc(S("in_high"), 1)

            def x_high(t):
                eng.wait_ge(S("xt_donein"), t + 1)
                for half in range(2):
                    ins = eng.copy(x0_high[:, 4 * half:4 * half + 4, t * P:(t + 1) * P],
                                   bank[3 + half][:, :].rearrange("p (c n) -> p c n", c=4))
                ins.then_inc(S("xt_actin"), 1)

            x_high(0)
            for p in range(KC):
                in_weights_high(p)
            for l in range(DEPTH):
                if l == 0:
                    for k in range(GROUPS[0]):
                        if k + 1 < NT:
                            x_high(k + 1)
                        eng.wait_ge(S("proj_done0"), k + 1)
                        if k >= 2:
                            eng.wait_ge(S("qkT_done"), k - 1)
                        j, t = k // NT, k % NT
                        b = bank[k % 2]
                        if j < 2:
                            cp = eng.copy(tok[:, k % 2, :], b[:, :])
                        else:
                            eng.copy(V0[:, t, :], b[:, F:2 * F])
                            cp = eng.copy(tok[:, k % 2, :].rearrange("p (h a d) -> p h a d", a=2, d=HD)[:, :, 0, :],
                                          b[:, 0:F].rearrange("p (h d) -> p h d", d=HD))
                        cp.then_inc(S(f"proj_free0{k % 2}"), 1)
                        if j < 2:
                            in_weights_high(KC * (j + 1) + 2 * t)
                            in_weights_high(KC * (j + 1) + 2 * t + 1)
                else:
                    eng.wait_ge(S("fz_abs"), 1)
                    eng.activation(fz[0:NH, 1, :], fz[0:NH, 1, :], ACT.Exp, scale=-1.0).then_inc(S("act_step"), 1)
                    eng.wait_ge(S("act_step"), 1)
                    eng.activation(fz[0:NH, 1, :], fz[0:NH, 1, :], ACT.Ln, bias=1.0).then_inc(S("fz_ln"), 1)
                    for g in range(4 * 4):
                        k = 2 * NT + g
                        if g == 2 * 4:
                            eng.wait_ge(S("cd_out"), 16)
                        if g % 2 == 0:
                            eng.wait_ge(S("proj_done1"), k + 1)
                            j, i = k // 4 - 2, k % 4
                            dst = QT[:, 4 * j + i, :] if j < 2 else KT[:, 4 * (j - 2) + i, :]
                            eng.copy(dst, bank[0][:, :]).then_inc(S("proj_free10"), 1)
                        if g + 2 < 4 * 4:
                            high_weights(g + 2)

                def expo(u):
                    hp, n, half = UNIT[u]
                    nk = P * (min(n, 1) + 1) + 1 if l == 0 else P * (n + 1)
                    eng.wait_ge(S(f"sp_ready{l}"), u + 1)
                    eng.activation(sp[:, u % 4, 0:nk], sp[:, u % 4, 0:nk], ACT.Exp, bias=nmax[:, u % 8:u % 8 + 1], scale=-1.0,
                                   accum_out=rsum[:, u % 8:u % 8 + 1]).then_inc(S(f"exp_done{l}"), 1)

                def out_weights_high(p):
                    w, high, _ = split(OUT_USE[l] + p // KC, p // KC, p % KC)
                    weights_here(eng, OUT_USE[l] + p // KC)
                    eng.copy(high, w).then_inc(S(f"out_high{l}"), 1)

                def out_high_part(k):
                    hp, n, _ = UNIT[2 * k]
                    eng.wait_ge(S(f"pv_done{l}"), 2 * k + 2)
                    eng.copy(attn_high[:, hp, n * P:(n + 1) * P], bank[5 + k % 2][:, 0:P]).then_inc(S(f"aT_high{l}"), 1)

                expo(0)
                expo(1)
                for u in range(UNITS):
                    if u + 2 < UNITS:
                        expo(u + 2)
                    if u % 4 == 3:
                        out_weights_high(u // 4)
                    hp, n, half = UNIT[u]
                    if half == 0:
                        nk = P * (min(n, 1) + 1) if l == 0 else P * (n + 1)
                        eng.wait_ge(S(f"pT_done{l}"), u + 1)
                        if u >= 2:
                            eng.wait_ge(S(f"pv_done{l}"), u - 1)
                        elif l == 0:
                            eng.wait_ge(S("zeros_free"), 1)
                        eng.copy(pT[:, u % 2, 0:nk], bank[3 + u % 2][:, 0:nk]).then_inc(S(f"pT_ready{l}0"), 1)
                        if u >= 2:
                            out_high_part(u // 2 - 1)
                out_high_part(UNITS // 2 - 1)

                for t in range(NT):
                    evac_x(f"{l}0", t)
                eng.wait_ge(S("shifted"), l + 1)
                eng.activation(pr, lg, ACT.Exp).then_inc(S("expd"), 1)

                def load_rows(e, b):
                    eng.dma_start(xe[0:CAP, b, :], xs_t[e]).then_inc(S(f"xe_in{l}{b}"), 16)

                def store_rows(e, b):
                    eng.wait_ge(S(f"y_dve{l}"), e + 1)
                    eng.wait_ge(S(f"y_act{l}"), e + 1)
                    eng.dma_start(ys_t[e], ysb[0:CAP, b, :]).then_inc(S(f"y_stored{l}{b}"), 16)

                def evac_rows(e, b):
                    eng.wait_ge(S(f"xeT_done{l}"), e + 1)
                    eng.copy(xeT[:, b, 0:4, :], bank[0][:, :].rearrange("p (c n) -> p c n", c=4)[:, :, 0:CAP]).then_inc(S(f"xeT_act{l}"), 1)

                def silu(e, b):
                    eng.wait_ge(S(f"gu_done{l}"), e + 1)
                    eng.activation(ssb[0:CAP, b, :], bank[2 + b][0:CAP, 0:F], ACT.Silu).then_inc(S(f"silu{l}"), 1)

                def evac_y(e, b, stored):
                    eng.wait_ge(S(f"y_done{l}"), e + 1)
                    if stored is not None:
                        eng.wait_ge(S(f"y_stored{l}{b}"), stored)
                    eng.copy(ysb[0:CAP, b, 0:BLK], bank[5][0:CAP, :]).then_inc(S(f"y_act{l}"), 1)

                def step(i, u, first=False, last=False):
                    e = 4 * i + u
                    silu(e, u % 2)
                    if not last:
                        evac_rows(e + 1, (u + 1) % 2)
                        if not isinstance(i, int) or e + 5 < NE:
                            load_rows(e + 5, (u + 1) % 4)
                    if not first:
                        started = not isinstance(i, int) or 4 * i + u - 1 >= 2
                        evac_y(e - 1, (u - 1) % 2, 32 * i + 16 * ((u - 1) // 2) if started else None)
                        store_rows(e - 1, (u - 1) % 2)

                eng.wait_ge(S(f"picked{l}"), 1)
                eng.copy(xe[0:CAP, 0, 0:BLK], bank[0][0:CAP, :]).then_inc(S(f"xe0_ready{l}"), 1)
                evac_rows(0, 0)
                eng.wait_ge(S(f"scattered{l}"), 16 * NT * TOPK)
                for b in range(1, 4):
                    load_rows(b, b)
                load_rows(4, 0)
                for u in range(3):
                    step(0, u, first=(u == 0))
                eng.wait_ge(S(f"picked{l}"), 2)
                for t in range(NT):
                    eng.activation(xres[:, t, :], xres[:, t, :], ACT.Copy, scale=ALPHA).then_inc(S(f"scaled{l}"), 1)
                with eng.Fori(0, NE // 4 - 2) as i:
                    for u in range(3, 7):
                        step(i, u)
                for u in range(3, 8):
                    step(NE // 4 - 2, u, last=(u == 7))
                evac_y(NE - 1, 1, 16 * ((NE - 1) // 2))
                store_rows(NE - 1, 1)
                n_ovf = eng.value_load(ovf_id[0:1, OVF:OVF + 1], min_val=0, max_val=OVF)
                with eng.If(n_ovf > 0):
                    eng.wait_ge(S(f"y_stored{l}0"), 16 * NE // 2)
                    with eng.Fori(0, OVF) as j:
                        eng.wait_ge(S(f"ov_turn{l}"), OV_STEPS * (j + 1) + 1)
                        eng.copy(xeT[:, 0, 0:4, :], bank[0][:, :].rearrange("p (c n) -> p c n", c=4)[:, :, 0:CAP]).then_inc(S(f"ov_turn{l}"), 1)
                        eng.wait_ge(S(f"ov_turn{l}"), OV_STEPS * (j + 1) + 4)
                        eng.activation(ssb[0:CAP, 0, :], bank[2][0:CAP, 0:F], ACT.Silu).then_inc(S(f"ov_turn{l}"), 1)
                        eng.wait_ge(S(f"ov_turn{l}"), OV_STEPS * (j + 1) + 9)
                        eng.copy(ysb[0:CAP, 0, 0:BLK], bank[5][0:CAP, :]).then_inc(S(f"ov_turn{l}"), 1)
                def state_high(t):
                    eng.wait_ge(S(f"xt_done{l}1"), t + 1)
                    for half in range(2):
                        ins = eng.copy(x1_high[:, 4 * half:4 * half + 4, t * P:(t + 1) * P],
                                       bank[3 + half][:, :].rearrange("p (c n) -> p c n", c=4))
                    ins.then_inc(S(f"xt_act{l}1"), 1)

                if l + 1 < DEPTH:
                    for p in range(2 * KC):
                        w, high, _ = split(IN_USE[1] + p // KC, p // KC, p % KC)
                        weights_here(eng, IN_USE[1] + p // KC)
                        eng.copy(high, w).then_inc(S("v_high"), 1)
                    eng.copy(wf_parts[:, 0, :, :], wf[:, :, :]).then_inc(S("v_high"), 1)
                    state_high(0)
                    for t in range(NT):
                        for b in range(2):
                            eng.wait_ge(S("proj_done1"), 2 * t + b + 1)
                            eng.copy(V[:, t, b * BLK:(b + 1) * BLK], bank[b][:, :]).then_inc(S(f"proj_free1{b}"), 1)
                            if b == (1 if t == 0 else 0) and t + 1 < NT:
                                state_high(t + 1)
                            if b == 0 and t == NT - 1:
                                high_weights(0)
                                high_weights(1)

        @block.vector
        def _(eng):
            link = chain(eng, "dve_step")

            def evac_x_tile(a, t):
                eng.wait_ge(S(f"xt_done{a}"), t + 1)
                eng.tensor_copy(xT[:, 4:8, t * P:(t + 1) * P], bank[4][:, :].rearrange("p (c n) -> p c n", c=4)).then_inc(S(f"xt_dve{a}"), 1)

            def low_weights(g):
                use = IN_USE[1] + 2 + g // 4
                eng.wait_ge(S("w_high"), g + 1)
                if g >= 2:
                    eng.wait_ge(S("proj_done1"), 2 * NT + g - 1)
                weights_here(eng, use)
                eng.tensor_tensor(wsplit[g % 2][:, 1, :, :], slot_in(use)[:, :, (g % 4) * P:(g % 4 + 1) * P],
                                  wsplit[g % 2][:, 0, :, :], ALU.subtract).then_inc(S("w_low"), 1)

            norms = [0]

            def half_stats(t, b):
                return eng.bn_stats(stats[:, t, b, :], xres[:, t, b * BLK:(b + 1) * BLK])

            def norm(l, w, t):
                v = xres[:, t, :]
                if t == 0:
                    norms[0] += 1
                    eng.wait_ge(S("ln_in"), 32 * norms[0])
                if w == 1:
                    half_stats(t, 0)
                    link(half_stats(t, 1))
                eng.bn_aggr(mv[:, t, :], stats[:, t, :, :].rearrange("p a b -> p (a b)")).then_inc(S(f"ln_stats{l}{w}"), 1)
                eng.wait_ge(S(f"ln_stats{l}{w}"), t + 1)
                link(eng.scalar_tensor_tensor(v, v, mv[:, t, 0:1], lnp[:, 0, :], ALU.subtract, ALU.mult))
                eng.wait_ge(S(f"rstd{l}{w}"), t + 1)
                eng.scalar_tensor_tensor(v, v, rstd[:, t:t + 1], lnp[:, 1, :], ALU.mult, ALU.add).then_inc(S(f"x_ready{l}{w}"), 1)

            def in_weights_low(p):
                w, high, low = split(p // KC, p // KC % 2, p % KC)
                eng.wait_ge(S("in_high"), p + 1)
                eng.tensor_tensor(low, w, high, ALU.subtract).then_inc(S("in_low"), 1)

            def x_low(t):
                eng.wait_ge(S("xt_actin"), t + 1)
                for half in range(2):
                    cols = slice(t * P, (t + 1) * P)
                    ins = eng.tensor_tensor(xlow[:, 4 * half:4 * half + 4, cols], bank[3 + half][:, :].rearrange("p (c n) -> p c n", c=4),
                                            x0_high[:, 4 * half:4 * half + 4, cols], ALU.subtract)
                ins.then_inc(S("xt_dvein"), 1)

            x_low(0)
            for p in range(KC):
                in_weights_low(p)
            eng.wait_ge(S("const_in"), 96)
            link(eng.tensor_scalar(sink[:, :], sink[:, :], -1.0, None, ALU.mult))
            for l in range(DEPTH):
                if l == 0:
                    def evac_heads(k):
                        eng.wait_ge(S("qkT_done"), k + 1)
                        j, t = k // NT, k % NT
                        dst = QT[:, 4 * j:4 * j + 4, :] if j < 2 else KT[:, 0:4, :]
                        eng.tensor_copy(dst[:, :, t * P:(t + 1) * P],
                                        bank[5 + k % 2][:, :].rearrange("p (h n) -> p h n", h=4)).then_inc(S("qkT_free"), 1)

                    for k in range(GROUPS[0]):
                        j, t = k // NT, k % NT
                        if k + 1 < NT:
                            x_low(k + 1)
                        eng.wait_ge(S(f"proj_free0{k % 2}"), k // 2 + 1)
                        if j < 2:
                            nh, hv = 8, tok[:, k % 2, :].rearrange("p (h d) -> p h d", d=HD)
                        else:
                            kd = tok[:, k % 2, :].rearrange("p (h a d) -> p h a d", a=2, d=HD)
                            nh, hv = 4, kd[:, :, 0, :]
                        r = hv[:, :, 0:ROT]
                        if k >= 1:
                            eng.wait_ge(S("roped"), k)
                        tc = rtmp[:, 0, 0:nh * ROT].rearrange("p (h d) -> p h d", h=nh)
                        ts = rtmp[:, 1, 0:nh * ROT].rearrange("p (h d) -> p h d", h=nh)
                        eng.tensor_tensor(tc, r, cs[:, t, 0, :].unsqueeze(1).to_broadcast([P, nh, ROT]), ALU.mult)
                        link(eng.tensor_tensor(ts, r, cs[:, t, 1, :].unsqueeze(1).to_broadcast([P, nh, ROT]), ALU.mult))
                        h = ROT // 2
                        rot = eng.tensor_tensor(hv[:, :, 0:h], tc[:, :, 0:h], ts[:, :, h:ROT], ALU.subtract)
                        if j < 2:
                            eng.tensor_tensor(hv[:, :, h:ROT], tc[:, :, h:ROT], ts[:, :, 0:h], ALU.add).then_inc(S("roped"), 1)
                        else:
                            link(eng.tensor_tensor(hv[:, :, h:ROT], tc[:, :, h:ROT], ts[:, :, 0:h], ALU.add))
                            eng.tensor_copy(kd[:, :, 1, :], kd[:, :, 0, :]).then_inc(S("roped"), 1)
                        if k >= 1:
                            evac_heads(k - 1)
                        if j < 2:
                            in_weights_low(KC * (j + 1) + 2 * t)
                            in_weights_low(KC * (j + 1) + 2 * t + 1)
                    evac_heads(GROUPS[0] - 1)
                else:
                    low_weights(0)
                    low_weights(1)
                    eng.wait_ge(S("forget"), 1)
                    z, az, ls, c = (fz[0:NH, k, :] for k in range(4))
                    link(eng.tensor_scalar(z, bank[7][0:NH, :], bf[:, 0:1], None, ALU.add))
                    link(eng.tensor_scalar(az, z, -1.0, None, ALU.mult))
                    eng.tensor_tensor(az, az, z, ALU.max).then_inc(S("fz_abs"), 1)
                    link(eng.tensor_scalar(z, z, 0.0, None, ALU.min))
                    eng.wait_ge(S("fz_ln"), 1)
                    link(eng.tensor_tensor(ls, z, az, ALU.subtract))
                    link(eng.memset(z, 0.0))
                    link(eng.tensor_tensor_scan(c, ls, z, 0.0, ALU.add, ALU.add))
                    eng.tensor_scalar(c, c, -1.0 / SCALE, None, ALU.mult).then_inc(S("decay"), 1)
                    for g in range(4 * 4):
                        k = 2 * NT + g
                        if g == 2 * 4 + 1:
                            eng.wait_ge(S("cd_out"), 16)
                        if g % 2 == 1:
                            eng.wait_ge(S("proj_done1"), k + 1)
                            j, i = k // 4 - 2, k % 4
                            dst = QT[:, 4 * j + i, :] if j < 2 else KT[:, 4 * (j - 2) + i, :]
                            eng.tensor_copy(dst, bank[1][:, :]).then_inc(S("proj_free11"), 1)
                        if g + 2 < 4 * 4:
                            low_weights(g + 2)

                def mask_and_max(u):
                    hp, n, half = UNIT[u]
                    h = 2 * hp + half
                    eng.wait_ge(S(f"s_done{l}"), u + 1)
                    if u >= 4:
                        eng.wait_ge(S(f"pT_done{l}"), u - 3)
                    s, o, m = s_bank(u), sp[:, u % 4, :], nmax[:, u % 8:u % 8 + 1]
                    if l == 0:
                        nk = P * (min(n, 1) + 1)
                        bias = band[:, :, :].rearrange("p a k -> p (a k)")[:, 2 * P - nk:2 * P]
                        eng.tensor_copy(o[:, nk:nk + 1], sink[:, h:h + 1])
                        eng.tensor_tensor_reduce(out=o[:, 0:nk], in0=s[:, 0:nk], in1=bias, scale=-SCALE,
                                                 scalar=sink[:, h:h + 1], op0=ALU.add, op1=ALU.min,
                                                 accum_out=m).then_inc(S("sp_ready0"), 1)
                    else:
                        if u % (2 * NT) == 0:
                            eng.wait_ge(S(f"cb_in{hp % 2}"), 16 * (hp // 2 + 1))
                        nk = P * (n + 1)
                        eng.tensor_tensor_reduce(out=o[:, 0:nk], in0=s[:, 0:nk], in1=cb[:, hp % 2, half, 0:nk],
                                                 scale=-SCALE, scalar=-NEG, op0=ALU.add, op1=ALU.min,
                                                 accum_out=m).then_inc(S("sp_ready1"), 1)

                def normalise(u):
                    hp, n, half = UNIT[u]
                    nk = P * (min(n, 1) + 1) if l == 0 else P * (n + 1)
                    eng.wait_ge(S(f"exp_done{l}"), u + 1)
                    link(eng.reciprocal(rinv[:, u % 8:u % 8 + 1], rsum[:, u % 8:u % 8 + 1]))
                    eng.tensor_scalar(sp[:, u % 4, 0:nk], sp[:, u % 4, 0:nk], rinv[:, u % 8:u % 8 + 1], None, ALU.mult).then_inc(S(f"p_ready{l}"), 1)

                def evac_out(k):
                    hp, n, _ = UNIT[2 * k]
                    eng.wait_ge(S(f"aT_high{l}"), k + 1)
                    eng.tensor_tensor(attn_low[:, hp, n * P:(n + 1) * P], bank[5 + k % 2][:, 0:P],
                                      attn_high[:, hp, n * P:(n + 1) * P], ALU.subtract).then_inc(S(f"aT_ready{l}"), 1)

                if l == 0:
                    eng.wait_ge(S("consts"), 1)
                mask_and_max(0)
                mask_and_max(1)
                normalise(0)
                for u in range(UNITS):
                    if u + 2 < UNITS:
                        mask_and_max(u + 2)
                    if u + 1 < UNITS:
                        normalise(u + 1)
                    hp, n, half = UNIT[u]
                    if half == 1:
                        nk = P * (min(n, 1) + 1) if l == 0 else P * (n + 1)
                        eng.wait_ge(S(f"pT_done{l}"), u + 1)
                        if u >= 2:
                            eng.wait_ge(S(f"pv_done{l}"), u - 1)
                        elif l == 0:
                            eng.wait_ge(S("zeros_free"), 1)
                        eng.tensor_copy(pT[:, u % 2, 0:nk], bank[3 + u % 2][:, 0:nk]).then_inc(S(f"pT_ready{l}1"), 1)
                    elif u >= 2:
                        evac_out(u // 2 - 1)
                evac_out(UNITS // 2 - 1)

                for t in range(NT):
                    for b in range(OUT_BLOCKS):
                        eng.wait_ge(S(f"wo_done{l}"), OUT_BLOCKS * t + b + 1)
                        v = xres[:, t, b * BLK:(b + 1) * BLK]
                        ins = eng.scalar_tensor_tensor(v, v, ALPHA, bank[b][:, :], ALU.mult, ALU.add)
                        ins.then_inc(S(f"res_done{l}"), 1)
                        if t >= 1 and b == 0:
                            evac_x_tile(f"{l}0", t - 1)
                        eng.wait_ge(S(f"res_done{l}"), OUT_BLOCKS * t + b + 1)
                        link(half_stats(t, b))
                    norm(l, 0, t)
                evac_x_tile(f"{l}0", NT - 1)

                def over(a, n):
                    return a.unsqueeze(2).to_broadcast([P, a.shape[1], n])

                def tiles(a):
                    return a.unsqueeze(1).to_broadcast([P, NT, a.shape[1]])

                mx, sm, rs, gm, kb, v1, k1, v2, k2, asn0 = (red[:, k, :] for k in range(10))
                eng.wait_ge(S(f"logits{l}"), NT)
                lps = bank[7][:, 0:NT * NE].rearrange("p (t e) -> p t e", t=NT)
                link(eng.tensor_tensor(lg, lps, tiles(br[:, :]), ALU.add))
                link(eng.tensor_reduce(mx, lg, X, ALU.max))
                eng.tensor_tensor(lg, lg, over(mx, NE), ALU.subtract).then_inc(S("shifted"), 1)
                eng.wait_ge(S("expd"), l + 1)
                link(eng.tensor_reduce(sm, pr, X, ALU.add))
                link(eng.reciprocal(rs, sm))
                link(eng.tensor_tensor(pr, pr, over(rs, NE), ALU.mult))
                eng.tensor_tensor(pair[:, :, :, 0:3], prg[:, :, :, 0:3], prg[:, :, :, 1:4], ALU.add)
                eng.tensor_tensor(pair[:, :, :, 3:5], prg[:, :, :, 0:2], prg[:, :, :, 2:4], ALU.add)
                link(eng.tensor_tensor(pair[:, :, :, 5:6], prg[:, :, :, 0:1], prg[:, :, :, 3:4], ALU.add))
                link(eng.tensor_reduce(gs, pair, X, ALU.max))
                link(eng.tensor_reduce(gm, gs, X, ALU.max))
                link(eng.tensor_tensor(gk, gs, over(gm, NG), ALU.is_equal))
                link(eng.tensor_tensor(gk, gk, tiles(w4[:, :]), ALU.mult))
                link(eng.tensor_reduce(kb, gk, X, ALU.max))
                link(eng.tensor_tensor(gk, gk, over(kb, NG), ALU.is_equal))
                link(eng.tensor_scalar(gs, gk, -1.0, None, ALU.add))
                mskg = msk.rearrange("p t (g e) -> p t g e", g=NG)
                link(eng.tensor_tensor(mskg, prg, gk.unsqueeze(3).to_broadcast([P, NT, NG, EPG]), ALU.mult))
                link(eng.tensor_tensor(mskg, mskg, gs.unsqueeze(3).to_broadcast([P, NT, NG, EPG]), ALU.add))
                for v, kk, oh in ((v1, k1, oh1), (v2, k2, oh2)):
                    link(eng.tensor_reduce(v, msk, X, ALU.max))
                    link(eng.tensor_tensor(tmp, msk, over(v, NE), ALU.is_equal))
                    link(eng.tensor_tensor(tmp, tmp, tiles(w16[:, :]), ALU.mult))
                    link(eng.tensor_reduce(kk, tmp, X, ALU.max))
                    link(eng.tensor_tensor(oh, tmp, over(kk, NE), ALU.is_equal))
                    if oh is oh1:
                        link(eng.tensor_scalar(tmp, oh1, -4.0, None, ALU.mult))
                        link(eng.tensor_tensor(msk, msk, tmp, ALU.add))
                eng.tensor_tensor(asn_b[:, :], oh1.rearrange("p t e -> p (t e)"), oh2.rearrange("p t e -> p (t e)"), ALU.add).then_inc(S("assigned"), 1)
                eng.tensor_tensor(asn0, oh1[:, :, 0], oh2[:, :, 0], ALU.add)
                link(eng.tensor_tensor(sm, v1, v2, ALU.add))
                link(eng.reciprocal(rs, sm))
                eng.tensor_tensor(gates[:, :, 0], v1, rs, ALU.mult)
                link(eng.tensor_tensor(gates[:, :, 1], v2, rs, ALU.mult))
                eng.wait_ge(S("ranked"), l + 1)
                eng.tensor_copy(tmp, bank[2][:, 0:NT * NE].rearrange("p (t e) -> p t e", t=NT))
                link(eng.tensor_copy(tot, bank[6][:, 0:NT * NE].rearrange("p (t e) -> p t e", t=NT)))
                for t in range(1, NT):
                    link(eng.tensor_tensor(tot[:, t, :], tot[:, t, :], tot[:, t - 1, :], ALU.add))
                link(eng.tensor_tensor(tmp[:, 1:NT, :], tmp[:, 1:NT, :], tot[:, 0:NT - 1, :], ALU.add))
                for t in range(NT):
                    ins = eng.tensor_scalar(picks[:, t, :], places[:, :], tmp[:, t, 0:1], asn0[:, t:t + 1], ALU.is_equal, ALU.mult)
                ins.then_inc(S("picks_ready"), 1)
                cnt = tot[:, NT - 1, :]
                link(eng.tensor_scalar(ext, cnt, float(CAP), None, ALU.is_gt))
                for m in range(2, (SEQ - 1) // CAP + 1):
                    link(eng.scalar_tensor_tensor(ext, cnt, float(m * CAP), ext, ALU.is_gt, ALU.add))
                link(eng.memset(dlt, 0.0))
                link(eng.tensor_tensor_scan(inc, ext, dlt, 0.0, ALU.add, ALU.add))
                link(eng.tensor_tensor(dlt, inc, ext, ALU.subtract))
                link(eng.tensor_scalar(dlt, dlt, float(CAP), float(CAP * (NE - 1)), ALU.mult, ALU.add))
                link(eng.tensor_tensor(dlt, dlt, e_cap[:, :], ALU.subtract))
                link(eng.tensor_scalar(slot, tmp, float(CAP), None, ALU.is_ge))
                link(eng.tensor_tensor(slot, slot, tiles(dlt), ALU.mult))
                link(eng.tensor_tensor(slot, slot, tmp, ALU.add))
                link(eng.tensor_tensor(slot, slot, tiles(e_cap[:, :]), ALU.add))
                link(eng.tensor_tensor(oh1, oh1, slot, ALU.mult))
                link(eng.tensor_tensor(oh2, oh2, slot, ALU.mult))
                link(eng.tensor_reduce(posf[:, :, 0], oh1, X, ALU.add))
                link(eng.tensor_reduce(posf[:, :, 1], oh2, X, ALU.add))
                eng.tensor_copy(pos[:, :, :], posf).then_inc(S("placed"), 1)
                row = cmpo[0:1]
                link(eng.tensor_tensor(row, inc[0:1].unsqueeze(1).to_broadcast([1, OVF, NE]),
                                       jo[0:1, :].unsqueeze(2).to_broadcast([1, OVF, NE]), ALU.is_le))
                link(eng.tensor_reduce(ids[0:1, 0:OVF], row, X, ALU.add))
                link(eng.tensor_scalar(ids[0:1, 0:OVF], ids[0:1, 0:OVF], float(NE - 1), None, ALU.min))
                link(eng.tensor_copy(ids[0:1, OVF:OVF + 1], inc[0:1, NE - 1:NE]))
                eng.tensor_copy(ovf_id[0:1, :], ids[0:1, :]).then_inc(S(f"routed{l}"), 1)
                eng.wait_ge(S(f"routed{l}"), 1)

                def evac_rows(e, b):
                    eng.wait_ge(S(f"xeT_done{l}"), e + 1)
                    eng.tensor_copy(xeT[:, b, 4:8, :], bank[1][:, :].rearrange("p (c n) -> p c n", c=4)[:, :, 0:CAP]).then_inc(S(f"xeT_dve{l}"), 1)

                def evac_hT(e, b):
                    eng.wait_ge(S(f"hT_done{l}"), e + 1)
                    eng.tensor_copy(hT[:, b, :, :], bank[4][:, 0:F].rearrange("p (c n) -> p c n", c=FC)[:, :, 0:CAP]).then_inc(S(f"hT_ready{l}"), 1)

                def times_up(e, b):
                    eng.wait_ge(S(f"silu{l}"), e + 1)
                    eng.tensor_tensor(hsb[0:CAP, b, :], ssb[0:CAP, b, :], bank[2 + b][0:CAP, F:2 * F], ALU.mult).then_inc(S(f"h_ready{l}"), 1)

                def evac_y(e, b, stored):
                    eng.wait_ge(S(f"y_done{l}"), e + 1)
                    if stored is not None:
                        eng.wait_ge(S(f"y_stored{l}{b}"), stored)
                    eng.tensor_copy(ysb[0:CAP, b, BLK:D], bank[6][0:CAP, :]).then_inc(S(f"y_dve{l}"), 1)

                def step(i, u, first=False, last=False):
                    e = 4 * i + u
                    if not first:
                        evac_hT(e - 1, (u - 1) % 2)
                    times_up(e, u % 2)
                    if not last:
                        evac_rows(e + 1, (u + 1) % 2)
                    if not first:
                        started = not isinstance(i, int) or 4 * i + u - 1 >= 2
                        evac_y(e - 1, (u - 1) % 2, 32 * i + 16 * ((u - 1) // 2) if started else None)

                eng.wait_ge(S(f"picked{l}"), 2)
                eng.tensor_copy(xe[0:CAP, 0, BLK:D], bank[1][0:CAP, :]).then_inc(S(f"xe0_ready{l}"), 1)
                evac_rows(0, 0)
                for u in range(3):
                    step(0, u, first=(u == 0))
                with eng.Fori(0, NE // 4 - 1) as i:
                    for u in range(3, 7):
                        step(i, u)
                step(NE // 4 - 1, 3, last=True)
                evac_hT(NE - 1, 1)
                evac_y(NE - 1, 1, 16 * ((NE - 1) // 2))
                n_ovf = eng.value_load(ovf_id[0:1, OVF:OVF + 1], min_val=0, max_val=OVF)
                with eng.If(n_ovf > 0):
                    eng.wait_ge(S(f"y_stored{l}0"), 16 * NE // 2)
                    with eng.Fori(0, OVF) as j:
                        eng.wait_ge(S(f"ov_turn{l}"), OV_STEPS * (j + 1) + 1)
                        eng.tensor_copy(xeT[:, 0, 4:8, :], bank[1][:, :].rearrange("p (c n) -> p c n", c=4)[:, :, 0:CAP]).then_inc(S(f"ov_turn{l}"), 1)
                        eng.wait_ge(S(f"ov_turn{l}"), OV_STEPS * (j + 1) + 5)
                        eng.tensor_tensor(hsb[0:CAP, 0, :], ssb[0:CAP, 0, :], bank[2][0:CAP, F:2 * F], ALU.mult).then_inc(S(f"ov_turn{l}"), 1)
                        eng.wait_ge(S(f"ov_turn{l}"), OV_STEPS * (j + 1) + 7)
                        eng.tensor_copy(hT[:, 0, :, :], bank[4][:, 0:F].rearrange("p (c n) -> p c n", c=FC)[:, :, 0:CAP]).then_inc(S(f"ov_turn{l}"), 1)
                        eng.wait_ge(S(f"ov_turn{l}"), OV_STEPS * (j + 1) + 9)
                        eng.tensor_copy(ysb[0:CAP, 0, BLK:D], bank[6][0:CAP, :]).then_inc(S(f"ov_turn{l}"), 1)
                def value_weights_low(first, end):
                    for p in range(first, end):
                        w, high, low = split(IN_USE[1] + p // KC, p // KC, p % KC)
                        eng.wait_ge(S("v_high"), p + 1)
                        eng.tensor_tensor(low, w, high, ALU.subtract).then_inc(S("v_low"), 1)

                def state_low(t):
                    eng.wait_ge(S(f"xt_act{l}1"), t + 1)
                    for half in range(2):
                        cols = slice(t * P, (t + 1) * P)
                        ins = eng.tensor_tensor(xlow[:, 4 * half:4 * half + 4, cols], bank[3 + half][:, :].rearrange("p (c n) -> p c n", c=4),
                                                x1_high[:, 4 * half:4 * half + 4, cols], ALU.subtract)
                    ins.then_inc(S(f"xt_dve{l}1"), 1)

                if l + 1 < DEPTH:
                    value_weights_low(0, KC)
                for t in range(NT):
                    eng.wait_ge(S(f"gy_in{l}{t % 2}"), 32 * (t // 2 + 1))
                    if t == 0:
                        eng.wait_ge(S(f"scaled{l}"), NT)
                    v = xres[:, t, :]
                    link(eng.scalar_tensor_tensor(v, gy[:, t % 2, 0, :], gates[:, t, 0:1], v, ALU.mult, ALU.add))
                    if l + 1 < DEPTH and t >= 2:
                        state_low(t - 1)
                    eng.scalar_tensor_tensor(v, gy[:, t % 2, 1, :], gates[:, t, 1:2], v, ALU.mult, ALU.add).then_inc(S(f"mixed{l}"), 1)
                    eng.wait_ge(S(f"mixed{l}"), t + 1)
                    norm(l, 1, t)
                    if l + 1 < DEPTH and t == 0:
                        value_weights_low(KC, KC + 3)
                        state_low(0)
                        value_weights_low(KC + 3, 2 * KC)
                if l + 1 < DEPTH:
                    state_low(NT - 1)
                    eng.wait_ge(S("v_high"), 2 * KC + 1)
                    eng.tensor_tensor(wf_parts[:, 1, :, :], wf[:, :, :], wf_parts[:, 0, :, :], ALU.subtract).then_inc(S("wf_low"), 1)


_INS = ["x", "ln_gain", "ln_bias", "swa_w_in", "swa_sinks", "swa_w_o", "fox_w_in", "fox_b_f", "fox_w_o",
        "w_router", "b_router", "w_gate", "w_up", "w_down"]


def kernel(**inputs):
    import numpy as np
    import concourse.bacc as bacc
    from concourse.bass_utils import run_bass_kernel_spmd

    half = ROT // 2
    inv_freq = np.power(np.float32(500000.0), -np.arange(half, dtype=np.float32) * np.float32(2.0 / ROT)).astype(np.float32)
    ang = np.arange(SEQ, dtype=np.float32)[:, None] * inv_freq[None, :]
    rope = np.stack([np.tile(np.cos(ang), 2), np.tile(np.sin(ang), 2)], axis=1).astype(np.float32)

    nc = bacc.Bacc("TRN2", target_bir_lowering=False, num_devices=1)
    arrays, args = {}, []
    for name in _INS:
        a = np.ascontiguousarray(inputs[name])
        arrays[f"in_{name}"] = a
        args.append(nc.dram_tensor(f"in_{name}", a.shape, mybir.dt.from_np(a.dtype), kind="ExternalInput").ap())
    arrays["rope"] = rope
    args.append(nc.dram_tensor("rope", rope.shape, mybir.dt.float32, kind="ExternalInput").ap())
    args.append(nc.dram_tensor("out", (1, SEQ, D), mybir.dt.float32, kind="ExternalOutput").ap())
    trunk(nc, *args)
    r = run_bass_kernel_spmd(nc, [arrays], core_ids=[0])
    return r.results[0]["out"]
```
